# Optimizing a Trainium2 kernel written in Bass

```python
import math
import jax, jax.numpy as jnp
from jax import lax
import numpy as np

D_MODEL = 2048
BATCH = 1
SEQ = 256
DEPTH = 1

HEAD_DIM = 128
NSA_HEADS = 8
NSA_KV_GROUPS = 2
NSA_HEADS_PER_GROUP = NSA_HEADS // NSA_KV_GROUPS
NSA_WIDTH = NSA_HEADS * HEAD_DIM
NSA_KV = NSA_KV_GROUPS * HEAD_DIM
NSA_BRANCHES = 3
CMP_BLOCK = 32
CMP_STRIDE = 16
CMP_HIDDEN = 512
SEL_BLOCK = 64
N_SELECT = 16
WINDOW = 512
DIFF_HEADS = 4
DIFF_QK_DIM = 128
DIFF_V_DIM = 2 * DIFF_QK_DIM
DIFF_WIDTH = DIFF_HEADS * DIFF_V_DIM
MIX_WIDTH = NSA_WIDTH + DIFF_WIDTH
IN_SIZES = (NSA_WIDTH,
            NSA_KV, NSA_KV,
            NSA_KV, NSA_KV,
            NSA_KV, NSA_KV,
            NSA_HEADS * NSA_BRANCHES,
            NSA_WIDTH,
            2 * DIFF_HEADS * DIFF_QK_DIM,
            2 * DIFF_HEADS * DIFF_QK_DIM,
            DIFF_WIDTH,
            DIFF_WIDTH)
IN_WIDTH = sum(IN_SIZES)
Q_BLOCK = 128
ROPE_THETA = 10000.0
NORM_EPS = 1e-6
SUBLN_EPS = 1e-5
NEG_INF = -1e30
FORCE_SCORE = 1e9

kernel_name = 'hymba_nsa_diffattn_hybrid'

def rms_norm(x, w, eps):
    xf = x.astype(jnp.float32)
    y = xf * lax.rsqrt(jnp.mean(xf * xf, axis=-1, keepdims=True) + eps)
    return (y * w.astype(jnp.float32)).astype(x.dtype)

def rope_tables(t_len, dim):
    pos = jnp.arange(t_len, dtype=jnp.float32)
    inv = ROPE_THETA ** (-jnp.arange(0, dim, 2, dtype=jnp.float32) / dim)
    ang = pos[:, None] * inv[None, :]
    return jnp.cos(ang), jnp.sin(ang)

def apply_rope(x, cos, sin):
    t_len, half = cos.shape
    bshape = (1, t_len) + (1,) * (x.ndim - 3) + (half,)
    c, s = cos.reshape(bshape), sin.reshape(bshape)
    xf = x.astype(jnp.float32)
    x1, x2 = xf[..., :half], xf[..., half:]
    return jnp.concatenate([x1 * c - x2 * s, x2 * c + x1 * s], axis=-1).astype(x.dtype)

def masked_softmax(s, mask):
    return jax.nn.softmax(jnp.where(mask, s, NEG_INF), axis=-1)

def compress_blocks(kv, pos_emb, w1, w2):
    b, t_len, g, dh = kv.shape
    n_cmp = (t_len - CMP_BLOCK) // CMP_STRIDE + 1
    idx = np.arange(n_cmp)[:, None] * CMP_STRIDE + np.arange(CMP_BLOCK)[None, :]
    blocks = kv[:, idx] + pos_emb[None, None, :, None, :].astype(kv.dtype)
    blocks = jnp.transpose(blocks, (0, 1, 3, 2, 4)).reshape(b, n_cmp, g, CMP_BLOCK * dh)
    return jax.nn.silu(blocks @ w1) @ w2

def cmp_to_sel_map(t_len):
    n_cmp = (t_len - CMP_BLOCK) // CMP_STRIDE + 1
    n_sel = t_len // SEL_BLOCK
    c0 = np.arange(n_cmp)[:, None] * CMP_STRIDE
    s0 = np.arange(n_sel)[None, :] * SEL_BLOCK
    ov = np.minimum(c0 + CMP_BLOCK, s0 + SEL_BLOCK) - np.maximum(c0, s0)
    return (np.maximum(ov, 0) / CMP_BLOCK).astype(np.float32)

def nsa_mixer(q, k_c, v_c, k_s, v_s, k_w, v_w, gate_logits, cmp_pos,
              cmp_k_w1, cmp_k_w2, cmp_v_w1, cmp_v_w2, cos, sin):
    b, t_len = q.shape[:2]
    g, hg, dh = NSA_KV_GROUPS, NSA_HEADS_PER_GROUP, HEAD_DIM
    scale = dh ** -0.5
    q = apply_rope(q.reshape(b, t_len, NSA_HEADS, dh), cos, sin).reshape(b, t_len, g, hg, dh)
    k_cmp = compress_blocks(apply_rope(k_c.reshape(b, t_len, g, dh), cos, sin), cmp_pos, cmp_k_w1, cmp_k_w2)
    v_cmp = compress_blocks(v_c.reshape(b, t_len, g, dh), cmp_pos, cmp_v_w1, cmp_v_w2)
    n_cmp = k_cmp.shape[1]
    cmp_end = jnp.arange(n_cmp) * CMP_STRIDE + CMP_BLOCK - 1
    n_sel_blocks = t_len // SEL_BLOCK
    n_top = min(N_SELECT, n_sel_blocks)
    sel_map = jnp.asarray(cmp_to_sel_map(t_len))
    blk_ids = jnp.arange(n_sel_blocks)
    sel_off = jnp.arange(SEL_BLOCK)
    ks_t = jnp.transpose(apply_rope(k_s.reshape(b, t_len, g, dh), cos, sin), (0, 2, 1, 3))
    vs_t = jnp.transpose(v_s.reshape(b, t_len, g, dh), (0, 2, 1, 3))
    b_idx = jnp.arange(b)[:, None, None, None]
    g_idx = jnp.arange(g)[None, :, None, None]
    pad = ((0, 0), (WINDOW, 0), (0, 0), (0, 0))
    kw_pad = jnp.pad(apply_rope(k_w.reshape(b, t_len, g, dh), cos, sin), pad)
    vw_pad = jnp.pad(v_w.reshape(b, t_len, g, dh), pad)
    gates = jax.nn.sigmoid(gate_logits.astype(jnp.float32)).reshape(b, t_len, g, hg, NSA_BRANCHES)

    def query_block(c):
        start = c * Q_BLOCK
        t = start + jnp.arange(Q_BLOCK)
        qc = lax.dynamic_slice_in_dim(q, start, Q_BLOCK, axis=1)
        s = jnp.einsum('bqghd,bngd->bghqn', qc, k_cmp).astype(jnp.float32) * scale
        m = cmp_end[None, :] <= t[:, None]
        p_cmp = masked_softmax(s, m) * m
        o_cmp = jnp.einsum('bghqn,bngd->bqghd', p_cmp.astype(v_cmp.dtype), v_cmp)
        imp = jnp.einsum('bghqn,nj->bgqj', p_cmp, sel_map)
        cur = t // SEL_BLOCK
        forced = (blk_ids[None, :] == 0) | (blk_ids[None, :] == cur[:, None]) | (blk_ids[None, :] == cur[:, None] - 1)
        imp = jnp.where(forced, FORCE_SCORE, imp)
        imp = jnp.where(blk_ids[None, :] > cur[:, None], NEG_INF, imp)
        _, top = lax.top_k(imp, n_top)
        tok = (top[..., None] * SEL_BLOCK + sel_off).reshape(b, g, Q_BLOCK, n_top * SEL_BLOCK)
        kg = ks_t[b_idx, g_idx, tok]
        vg = vs_t[b_idx, g_idx, tok]
        s = jnp.einsum('bqghd,bgqkd->bghqk', qc, kg).astype(jnp.float32) * scale
        m = (tok <= t[None, None, :, None])[:, :, None]
        p = masked_softmax(s, m)
        o_sel = jnp.einsum('bghqk,bgqkd->bqghd', p.astype(vg.dtype), vg)
        kwc = lax.dynamic_slice_in_dim(kw_pad, start, WINDOW + Q_BLOCK, axis=1)
        vwc = lax.dynamic_slice_in_dim(vw_pad, start, WINDOW + Q_BLOCK, axis=1)
        spos = start - WINDOW + jnp.arange(WINDOW + Q_BLOCK)
        m = (spos[None, :] <= t[:, None]) & (spos[None, :] > t[:, None] - WINDOW) & (spos[None, :] >= 0)
        s = jnp.einsum('bqghd,bkgd->bghqk', qc, kwc).astype(jnp.float32) * scale
        p = masked_softmax(s, m)
        o_win = jnp.einsum('bghqk,bkgd->bqghd', p.astype(vwc.dtype), vwc)
        gc = lax.dynamic_slice_in_dim(gates, start, Q_BLOCK, axis=1)
        o = gc[..., 0:1] * o_cmp + gc[..., 1:2] * o_sel + gc[..., 2:3] * o_win
        return o.astype(q.dtype)

    out = lax.map(query_block, jnp.arange(t_len // Q_BLOCK))
    return jnp.transpose(out, (1, 0, 2, 3, 4, 5)).reshape(b, t_len, NSA_WIDTH)

def diff_mixer(q, k, v, lam_q1, lam_k1, lam_q2, lam_k2, subln_w, lambda_init, cos, sin):
    b, t_len = q.shape[:2]
    scale = DIFF_QK_DIM ** -0.5
    q = apply_rope(q.reshape(b, t_len, 2, DIFF_HEADS, DIFF_QK_DIM), cos, sin)
    k = apply_rope(k.reshape(b, t_len, 2, DIFF_HEADS, DIFF_QK_DIM), cos, sin)
    v = v.reshape(b, t_len, DIFF_HEADS, DIFF_V_DIM)
    f32 = jnp.float32
    lam = (jnp.exp(jnp.sum(lam_q1.astype(f32) * lam_k1.astype(f32)))
           - jnp.exp(jnp.sum(lam_q2.astype(f32) * lam_k2.astype(f32))) + lambda_init)
    kpos = jnp.arange(t_len)

    def query_block(c):
        start = c * Q_BLOCK
        t = start + jnp.arange(Q_BLOCK)
        qc = lax.dynamic_slice_in_dim(q, start, Q_BLOCK, axis=1)
        s = jnp.einsum('bqshd,bkshd->bshqk', qc, k).astype(f32) * scale
        p = masked_softmax(s, kpos[None, :] <= t[:, None])
        a = p[:, 0] - lam * p[:, 1]
        return jnp.einsum('bhqk,bkhd->bqhd', a.astype(v.dtype), v)

    out = lax.map(query_block, jnp.arange(t_len // Q_BLOCK))
    out = jnp.transpose(out, (1, 0, 2, 3, 4)).reshape(b, t_len, DIFF_HEADS, DIFF_V_DIM)
    out = rms_norm(out, subln_w, SUBLN_EPS) * (1.0 - lambda_init)
    return out.reshape(b, t_len, DIFF_WIDTH)

def setup_inputs(seed: int = 0) -> dict:
    key = jax.random.key(seed)
    ks = jax.random.split(key, 16)
    f32 = jnp.float32
    nrm = lambda k, shape, s: jax.random.normal(k, shape, f32) * s
    return {
        'x': nrm(ks[0], (BATCH, SEQ, D_MODEL), 1.0),
        'norm_w': 1.0 + nrm(ks[1], (DEPTH, D_MODEL), 0.01),
        'w_in': nrm(ks[2], (DEPTH, D_MODEL, IN_WIDTH), D_MODEL ** -0.5),
        'cmp_pos': nrm(ks[3], (DEPTH, CMP_BLOCK, HEAD_DIM), 0.1),
        'cmp_k_w1': nrm(ks[4], (DEPTH, CMP_BLOCK * HEAD_DIM, CMP_HIDDEN), (CMP_BLOCK * HEAD_DIM) ** -0.5),
        'cmp_k_w2': nrm(ks[5], (DEPTH, CMP_HIDDEN, HEAD_DIM), CMP_HIDDEN ** -0.5),
        'cmp_v_w1': nrm(ks[6], (DEPTH, CMP_BLOCK * HEAD_DIM, CMP_HIDDEN), (CMP_BLOCK * HEAD_DIM) ** -0.5),
        'cmp_v_w2': nrm(ks[7], (DEPTH, CMP_HIDDEN, HEAD_DIM), CMP_HIDDEN ** -0.5),
        'lam_q1': nrm(ks[8], (DEPTH, DIFF_QK_DIM), 0.1),
        'lam_k1': nrm(ks[9], (DEPTH, DIFF_QK_DIM), 0.1),
        'lam_q2': nrm(ks[10], (DEPTH, DIFF_QK_DIM), 0.1),
        'lam_k2': nrm(ks[11], (DEPTH, DIFF_QK_DIM), 0.1),
        'subln_w': 1.0 + nrm(ks[12], (DEPTH, DIFF_V_DIM), 0.01),
        'w_out': nrm(ks[13], (DEPTH, MIX_WIDTH, D_MODEL), MIX_WIDTH ** -0.5),
        'final_norm_w': 1.0 + nrm(ks[14], (D_MODEL,), 0.01),
    }

def reference(x, norm_w, w_in, cmp_pos, cmp_k_w1, cmp_k_w2, cmp_v_w1, cmp_v_w2,
              lam_q1, lam_k1, lam_q2, lam_k2, subln_w, w_out, final_norm_w):
    t_len = x.shape[1]
    cos, sin = rope_tables(t_len, HEAD_DIM)
    split_points = np.cumsum(IN_SIZES)[:-1].tolist()
    for l in range(DEPTH):
        lambda_init = 0.8 - 0.6 * math.exp(-0.3 * l)
        h = rms_norm(x, norm_w[l], NORM_EPS)
        proj = h @ w_in[l]
        (q_a, kc_a, vc_a, ks_a, vs_a, kw_a, vw_a, g_a, z_a,
         q_b, k_b, v_b, z_b) = jnp.split(proj, split_points, axis=-1)
        o_a = nsa_mixer(q_a, kc_a, vc_a, ks_a, vs_a, kw_a, vw_a, g_a, cmp_pos[l],
                        cmp_k_w1[l], cmp_k_w2[l], cmp_v_w1[l], cmp_v_w2[l], cos, sin)
        o_b = diff_mixer(q_b, k_b, v_b, lam_q1[l], lam_k1[l], lam_q2[l], lam_k2[l],
                         subln_w[l], lambda_init, cos, sin)
        mixed = jnp.concatenate([o_a * jax.nn.silu(z_a), o_b * jax.nn.silu(z_b)], axis=-1)
        x = x + mixed @ w_out[l]
    return rms_norm(x, final_norm_w, NORM_EPS)


_drawn_inputs = setup_inputs


def setup_inputs(seed=0):
    import zlib

    import numpy as np

    out = dict(_drawn_inputs(seed))
    spreads = {}
    factors = {'norm_w': 8.0,
     'cmp_pos': 5.129,
     'lam_q1': 2.807,
     'lam_k1': 3.762,
     'lam_q2': 2.878,
     'subln_w': 8.0,
     'final_norm_w': 5.568}
    for name, (base, spread) in spreads.items():
        noise = np.random.default_rng([zlib.crc32(name.encode()), seed]).standard_normal(out[name].shape)
        drawn = base * np.exp(spread * noise) if base else spread * noise
        out[name] = __import__('jax').numpy.asarray(drawn.astype(out[name].dtype))
    for name, factor in factors.items():
        out[name] = (out[name] * factor).astype(out[name].dtype)
    return out
```

```python
from contextlib import ExitStack

import numpy as np

import concourse.bass as bass
from concourse import mybir

P = 128
D_MODEL, SEQ, HEAD = 2048, 256, 128
TT = SEQ // P
KT = D_MODEL // P
CH = 4
NB = 512
CMP_BLOCK, CMP_STRIDE, CMP_HIDDEN = 32, 16, 512
N_CMP = (SEQ - CMP_BLOCK) // CMP_STRIDE + 1
NC = 16
SCALE = float(HEAD) ** -0.5
NEG = -1e30
NORM_EPS, SUBLN_EPS = 1e-6, 1e-5
LAMBDA_INIT = 0.8 - 0.6
THETA = 10000.0

COLS = {}
_at = 0
for _n, _w in (("qa", 1024), ("kc", 256), ("vc", 256), ("ks", 256), ("vs", 256), ("kw", 256), ("vw", 256),
               ("gate", 24), ("za", 1024), ("qb", 1024), ("kb", 1024), ("vb", 1024), ("zb", 1024)):
    COLS[_n] = (_at, _w)
    _at += _w
IN_WIDTH = _at
N_GATE = 24
BLOCKS = [("kc", "vc"), ("ks", "kw"), ("vs", "vw"), ("qa", 0), ("qa", 1), ("qb", 0), ("kb", 0), ("qb", 1),
          ("kb", 1), ("vb", 0), ("vb", 1), ("za", 0), ("za", 1), ("zb", 0), ("zb", 1)]
N_IN = len(BLOCKS)
N_OUT = D_MODEL // NB
STREAM = [("in", b, j) for b in (0, 1) for j in range(KT // CH)]
_cmp = [(w, 0, j) for w in ("ck", "cv") for j in range(CMP_BLOCK // CH)]
for _b in range(2, 6):
    for _j in range(KT // CH):
        STREAM += [("in", _b, _j), _cmp[(_b - 2) * 4 + _j]]
STREAM += [("in", b, j) for b in range(6, N_IN) for j in range(KT // CH)]
STREAM += [("out", n, j) for n in range(N_OUT) for j in range(KT // CH)]
N_CHUNKS = len(STREAM)
LAST = {s[:2]: c for c, s in enumerate(STREAM)}

ROPE = [0, 1, 3, 4, 5, 6, 7, 8]
HEADS_AT = {0: 5, 1: 9, 3: 24, 4: 32, 5: 42, 6: 46, 7: 50, 8: 54}
UNIT_AT = [40, 44, 48, 52, 56, 60]
N_UNITS = len(UNIT_AT)
N_A = 4
RAW, SPLIT = 4, 3

C_COS, C_SIN, C_ID, C_CADD, C_C01, C_SEL, C_HM, C_HALF = 0, 128, 256, 384, 416, 448, 480, 488
C_N = 492


def unit_a(u):
    return u // 2, 1 + u % 2


def program(nc, stream, w_gate, xT, x, norm_w, cmp_pos, ck_w2, cv_w2, lam, subln_w, final_w, consts, out):
    f32, f32r, bf16 = mybir.dt.float32, mybir.dt.float32r, mybir.dt.bfloat16
    ALU, ACT, AX = mybir.AluOpType, mybir.ActivationFunctionType, mybir.AxisListType

    with ExitStack() as ctx:
        base = (nc.sbuf_base + 31) // 32 * 32
        top = [base]

        def region(n):
            top[0] += n
            return top[0] - n

        def sb(name, shape, dt=f32, at=None):
            n = int(np.prod(shape[1:])) * (2 if dt == bf16 else 4)
            return nc.alloc_sbuf_tensor_at(name, shape, dt, offset=region((n + 31) // 32 * 32) if at is None else at)

        x_nat = sb("x_nat", [P, TT, D_MODEL])
        hT = [sb("hT_hi", [P, KT, SEQ], f32r), sb("hT_lo", [P, KT, SEQ], f32r)]
        raw = sb("raw", [P, RAW, CH * NB])
        whi = sb("whi", [P, SPLIT, CH * NB], f32r)
        wlo = sb("wlo", [P, SPLIT, CH * NB], f32r)
        r1, r2, r3 = region(32768), region(16384), region(8192)
        r_e, r_p = region(6144), region(6144)
        r_s = region(8192)
        stage = sb("stage", [P, TT, NB], at=r_s)
        stage2 = sb("stage2", [P, TT, NB], at=r_s + 4096)
        sq = sb("sq", [P, D_MODEL], at=r_s)
        const = sb("const", [P, C_N])
        const16 = sb("const16", [P, 2 * P], bf16)
        small = sb("small", [P, 64])
        gate = sb("gate", [P, TT, N_GATE])
        kcmpT = sb("kcmpT", [P, 2 * NC])
        nw = sb("nw", [P, KT])
        BLK = CMP_BLOCK * 64 + 64
        blk = {"ck": sb("kblk", [P, BLK], f32r, at=r1), "cv": sb("vblk", [P, BLK], f32r, at=r1 + 4 * BLK)}
        r1b = r1 + 8 * BLK
        blkf = {"ck": sb("kblkf", [P, CMP_BLOCK, 2, NC], at=r1b), "cv": sb("vblkf", [P, CMP_BLOCK, 2, NC], at=r1 + 24576)}
        hid = sb("hid", [64, CMP_HIDDEN], at=r1b)
        hidT = sb("hidT", [P, 4, 2 * NC], at=r1b + 2048)
        hidT8 = sb("hidT8", [P, 4, 8, NC], at=r1b + 2560)
        gT = sb("gT", [64, SEQ], at=r1b + 4608)
        qbT = sb("qbT", [P, 8, SEQ], at=r1)
        kbT = sb("kbT", [P, 8, SEQ], at=r1 + 8192)
        vb = sb("vb", [P, TT, 1024], at=r1 + 16384)
        ob = sb("ob", [P, TT, 1024], at=r1 + 24576)
        vbd = sb("vbd", [P, 8, P], at=r1 + 24576)
        pcT = sb("pcT", [P, TT, P], at=r1 + 24576 + 4096)
        cs = sb("cs", [P, TT, 8, NC], at=r1 + 24576 + 5120)
        ce = sb("ce", [P, TT, 8, NC], at=r1 + 24576 + 6144)
        fw = sb("fw", [P, D_MODEL], at=r1 + 16384)
        xTs = sb("xTs", [P, KT, SEQ], at=r2)
        qaT = sb("qaT", [P, 8, SEQ], at=r2)
        kaT = sb("kaT", [P, 4, SEQ], at=r2 + 8192)
        va = sb("va", [P, TT, NB], at=r2 + 12288)
        subw = sb("subw", [P, 2 * HEAD], at=r2 + 15360)
        mixT = [[sb("mixA_hi", [P, 8, SEQ], f32r, at=r2), sb("mixA_lo", [P, 8, SEQ], f32r, at=r2 + 8192)],
                [sb("mixB_hi", [P, 8, SEQ], f32r, at=r1), sb("mixB_lo", [P, 8, SEQ], f32r, at=r1 + 8192)]]
        w2 = {"ck": sb("w2k", [P, 4, HEAD], at=r3), "cv": sb("w2v", [P, 4, HEAD], at=r3 + 2048)}
        lamv = sb("lamv", [P, 4, HEAD], at=r3 + 4096)
        lamp = sb("lamp", [P, 2, HEAD], at=r3 + 6144)
        oaT = sb("oaT", [P, TT, 8, P], at=r3)
        e0 = sb("e0", [P, 4, P], at=r_e)
        e1 = sb("e1", [P, 4, SEQ], at=r_e + 2048)
        gwf = sb("gwf", [P, KT, N_GATE], at=r_e)
        gw = sb("gw", [P, KT * 64 + 64], f32r, at=r_e + 4 * KT * N_GATE)
        pT = sb("pT", [P, 3, NB], at=r_p)
        junk = sb("junk", [P, 2, NB], at=r_p)
        kvcT = sb("kvcT", [P, 4, SEQ], at=r_p)
        assert top[0] <= nc.sbuf_usable_end, (top[0], nc.sbuf_usable_end)

        cos = const[:, C_COS:C_COS + 128].rearrange("p (t d) -> p t d", t=TT)
        sin = const[:, C_SIN:C_SIN + 128].rearrange("p (t d) -> p t d", t=TT)
        ident = const[:, C_ID:C_ID + 128]
        cadd = const[:, C_CADD:C_CADD + 32].rearrange("p (t n) -> p t n", t=TT)
        c01 = const[:, C_C01:C_C01 + 32].rearrange("p (t n) -> p t n", t=TT)
        sel = const[0:64, C_SEL:C_SEL + 32]
        headmask = const[:, C_HM:C_HM + 8]
        half = const[:, C_HALF:C_HALF + 4]
        ident16, mask16 = const16[:, 0:P], const16[:, P:2 * P]
        rstd, nrstd, ssq = small[:, 0:2], small[:, 2:4], small[:, 4:6]
        nmax, sums, coef = small[:, 6:14], small[:, 14:22], small[:, 22:30]
        nlam, lamd = small[:, 30:31], small[:, 32:34]
        ssb, rsb = small[:, 34:38], small[:, 38:42]
        ssy, rsy = small[:, 42:50], small[:, 50:52]
        ssyt = small[:, 52:54]
        posT = sb("posT", [P, CMP_BLOCK])
        cstat = sb("cstat", [P, 2, TT * 8])
        assert top[0] <= nc.sbuf_usable_end, (top[0], nc.sbuf_usable_end)

        def bank(name, n=1):
            return ctx.enter_context(nc.psum_tensor(name, [P, n, NB] if n > 1 else [P, NB], f32))

        acc = [bank(f"acc{i}") for i in range(3)]
        S = bank("S", 3)
        O = bank("O", 2)

        def sem(name):
            return ctx.enter_context(nc.semaphore(name))

        raw_in = [sem(f"raw_in{i}") for i in range(RAW)]
        hi_ready, lo_ready = sem("hi_ready"), sem("lo_ready")
        chunk_used = sem("chunk_used")
        xT_in = [sem(f"xT_in{i}") for i in range(4)]
        nw_in, x_in, const_in, subw_in, fw_in, w2_in, gw_in, lam_in = (
            sem(n) for n in ("nw_in", "x_in", "const_in", "subw_in", "fw_in", "w2_in", "gw_in", "lam_in"))
        h_scaled, h_hi, h_lo = sem("h_scaled"), sem("h_hi"), sem("h_lo")
        x_squared, rstd_steps, tables = sem("x_squared"), sem("rstd_steps"), sem("tables")
        acc_done = sem("acc_done")
        acc_read = {"v": sem("acc_read_v"), "s": sem("acc_read_s")}
        rope_ready = sem("rope_ready")
        heads_turned, heads_taken = sem("heads_turned"), sem("heads_taken")
        mask_ready = sem("mask_ready")
        blk_zero, blk_sum, blk_hi, blk_lo = sem("blk_zero"), sem("blk_sum"), sem("blk_hi"), sem("blk_lo")
        hid_done, hid_taken, hid_turned, hid_act = (sem(n) for n in ("hid_done", "hid_taken", "hid_turned", "hid_act"))
        cmp_out, kcmp_ready, vbd_ready = sem("cmp_out"), sem("kcmp_ready"), sem("vbd_ready")
        gw_hi, gw_lo, g_done, g_taken, g_turned, g_exp, gates_ready = (
            sem(n) for n in ("gw_hi", "gw_lo", "g_done", "g_taken", "g_turned", "g_exp", "gates_ready"))
        lam_sums, lam_exp = sem("lam_sums"), sem("lam_exp")
        scores_done, max_ready, exp_done, probs_ready = (
            sem(n) for n in ("scores_done", "max_ready", "exp_done", "probs_ready"))
        probs_turned, pT_ready, pv_done, o_taken = (
            sem(n) for n in ("probs_turned", "pT_ready", "pv_done", "o_taken"))
        cs_done, cs_masked, cs_shift, ce_done, pc_ready, pc_turned, pcT_ready = (
            sem(n) for n in ("cs_done", "cs_masked", "cs_shift", "ce_done", "pc_ready", "pc_turned", "pcT_ready"))
        ob_squared, ob_rstd, ob_ready = (sem(n) for n in ("ob_squared", "ob_rstd", "ob_ready"))
        z_ready, zb_ready, z_turned, mix_f, mix_hi, mix_lo = (
            sem(n) for n in ("z_ready", "zb_ready", "z_turned", "mix_f", "mix_hi", "mix_lo"))
        y_squared, yw_ready, y_sum, y_rstd, y_out_s, y_out_v = (
            sem(n) for n in ("y_squared", "yw_ready", "y_sum", "y_rstd", "y_out_s", "y_out_v"))
        stored, vstep, pstep = sem("stored"), sem("vstep"), sem("pstep")

        READERS = {b: "v" for b in range(N_IN + N_OUT)}
        READERS.update({0: "vs", 2: "s", 9: "s", 10: "s", 11: "s", 12: "s", 13: "s", 14: "s"})

        def reads(engine, uses):
            return sum(engine in READERS[n // TT] for n in range(uses))

        def block_of(c):
            kind, b, _ = STREAM[c]
            return b if kind == "in" else N_IN + b

        def ends(c):
            return c in LAST.values()

        def wait_used(eng, c):
            if c in (LAST["ck", 0], LAST["cv", 0]):
                eng.wait_ge(hid_done, 1 + (STREAM[c][0] == "cv"))
            elif ends(c):
                eng.wait_ge(acc_done, TT * (block_of(c) + 1))
            else:
                eng.wait_ge(chunk_used, sum(not ends(i) for i in range(c + 1)))

        block = ctx.enter_context(nc.Block())

        @block.sync
        def _(sp):
            for i in range(RAW):
                sp.dma_start(xTs[:, CH * i:CH * i + CH, :], xT[:, CH * i:CH * i + CH, :]).then_inc(xT_in[i], 16)
                sp.dma_start(raw[:, i, :], stream[i, :, :]).then_inc(raw_in[i], 16)
            with sp.Fori(1, N_CHUNKS // RAW) as r:
                for i in range(RAW):
                    sp.wait_ge(hi_ready, RAW * r + (i + 1 - RAW))
                    sp.wait_ge(lo_ready, RAW * r + (i + 1 - RAW))
                    sp.dma_start(raw[:, i, :], stream[bass.ds(RAW * r + i, 1)].rearrange("c p n -> (c p) n")).then_inc(raw_in[i], 16)
            for t in range(TT):
                sp.wait_ge(y_out_s, t + 1)
                sp.wait_ge(y_out_v, t + 1)
                sp.dma_start(out[t * P:(t + 1) * P, :], x_nat[:, t, :]).then_inc(stored, 16)
            sp.wait_ge(stored, 16 * TT)

        @block.gpsimd
        def _(pool):
            def link(ins):
                link.n += 1
                ins.then_inc(pstep, 1)
                pool.wait_ge(pstep, link.n)
            link.n = 0

            pool.memset(const16[:, :], 0.0).then_inc(mask_ready, 1)
            pool.wait_ge(mask_ready, 1)
            pool.affine_select(out=ident16, in_=ident16, compare_op=ALU.not_equal, fill=1.0, base=0,
                               pattern=[[-1, P]], channel_multiplier=1).then_inc(mask_ready, 1)
            pool.affine_select(out=mask16, in_=mask16, compare_op=ALU.is_ge, fill=NEG, base=0,
                               pattern=[[-1, P]], channel_multiplier=1).then_inc(mask_ready, 1)
            for w in ("ck", "cv"):
                pool.memset(blkf[w][:, :, :, N_CMP:NC], 0.0).then_inc(blk_zero, 1)
                pool.memset(blk[w][:, CMP_BLOCK * 64:BLK].bitcast(f32), 0.0).then_inc(blk_zero, 1)
            pool.memset(gw[:, :].bitcast(f32), 0.0).then_inc(blk_zero, 1)

            pool.wait_ge(const_in, 32)
            pool.wait_ge(x_squared, TT)
            link(pool.tensor_scalar(ssq, ssq, 1.0 / D_MODEL, NORM_EPS, ALU.mult, ALU.add))
            pool.tensor_tensor(rstd, ssq, half[:, 0:2], ALU.pow).then_inc(rstd_steps, 1)
            pool.wait_ge(rstd_steps, 1)
            pool.tensor_scalar(nrstd, rstd, -1.0, 0.0, ALU.mult, ALU.add).then_inc(rstd_steps, 1)

            def rope_sum(b):
                w = 2 * HEAD if b == 0 else NB
                for t in range(TT):
                    pool.wait_ge(acc_read["v"], reads("v", TT * b + t + 1))
                    pool.tensor_tensor(stage[:, t, 0:w], stage[:, t, 0:w], stage2[:, t, 0:w], ALU.add)\
                        .then_inc(rope_ready, 1)

            def head_norm(u):
                k = u - N_A
                f = (1.0 - LAMBDA_INIT) ** -2
                pool.wait_ge(ob_squared, 4 * (k + 1))
                if k:
                    pool.wait_ge(ob_ready, 4 * k)
                link(pool.tensor_scalar(rsb, ssb, f / (2 * HEAD), SUBLN_EPS * f, ALU.mult, ALU.add))
                pool.tensor_tensor(rsb, rsb, half, ALU.pow).then_inc(ob_rstd, 1)

            for b in ROPE:
                rope_sum(b)
            for u in range(N_A, N_UNITS):
                head_norm(u)
            pool.wait_ge(fw_in, 16)
            for n in range(N_OUT - 1):
                for t in range(TT):
                    pool.wait_ge(acc_read["v"], reads("v", TT * (N_IN + n) + t + 1))
                    pool.wait_ge(y_squared, TT * n + t + 1)
                    y = x_nat[:, t, n * NB:(n + 1) * NB]
                    pool.tensor_tensor(y, y, fw[:, n * NB:(n + 1) * NB], ALU.mult).then_inc(yw_ready, 1)
            for t in range(TT):
                pool.wait_ge(y_sum, t + 1)
                link(pool.tensor_scalar(rsy[:, t:t + 1], ssyt[:, t:t + 1], 1.0 / D_MODEL, NORM_EPS, ALU.mult, ALU.add))
                pool.tensor_tensor(rsy[:, t:t + 1], rsy[:, t:t + 1], half[:, 0:1], ALU.pow).then_inc(y_rstd, 1)

        @block.scalar
        def _(act):
            act.dma_start(nw[:, :], norm_w).then_inc(nw_in, 16)

            def split_hi(c):
                act.wait_ge(raw_in[c % RAW], 16 * (c // RAW + 1))
                if c >= SPLIT:
                    wait_used(act, c - SPLIT)
                act.activation(whi[:, c % SPLIT, :], raw[:, c % RAW, :], ACT.Copy).then_inc(hi_ready, 1)

            def h_hi_part(i):
                act.wait_ge(h_scaled, i + 1)
                act.activation(hT[0][:, CH * i:CH * i + CH, :], xTs[:, CH * i:CH * i + CH, :], ACT.Copy)\
                    .then_inc(h_hi, 1)

            def use_done(b, t):
                act.wait_ge(acc_done, TT * b + t + 1)
                return acc[(TT * b + t) % 3]

            def take_vc():
                for t in range(TT):
                    a = use_done(0, t)
                    act.activation(stage[:, t, NB // 2:NB], a[:, NB // 2:NB], ACT.Copy, scale=rstd[:, t:t + 1])\
                        .then_inc(acc_read["s"], 1)

            def take_v(b):
                for t in range(TT):
                    a = use_done(b, t)
                    dst = va[:, t, :] if b == 2 else vb[:, t, (b - 9) * NB:(b - 8) * NB]
                    act.activation(dst, a[:, :], ACT.Copy, scale=rstd[:, t:t + 1]).then_inc(acc_read["s"], 1)

            def take_heads(b):
                n = ROPE.index(b)
                dst = {0: kvcT[:, :, :], 1: kaT[:, :, :], 3: qaT[:, 0:4, :], 4: qaT[:, 4:8, :], 5: qbT[:, 0:4, :],
                       6: kbT[:, 0:4, :], 7: qbT[:, 4:8, :], 8: kbT[:, 4:8, :]}[b]
                for t in range(TT):
                    act.wait_ge(heads_turned, TT * n + t + 1)
                    act.activation(dst[:, :, t * P:(t + 1) * P], S[:, 1 + t, :].rearrange("p (h q) -> p h q", h=4),
                                   ACT.Copy, scale=SCALE if b in (3, 4, 5, 7) else 1.0).then_inc(heads_taken, 1)

            def take_hid(k):
                act.wait_ge(hid_done, k + 1)
                if k:
                    act.wait_ge(hid_turned, k)
                act.activation(hid[:, :], O[0:64, k, :], ACT.Copy).then_inc(hid_taken, 1)

            def silu_hid(k):
                act.wait_ge(hid_turned, k + 1)
                src = O[:, 0, 0:4 * 2 * NC].rearrange("p (k g n) -> p k g n", k=4, g=2)
                if k == 0:
                    act.activation(hidT[:, :, :], O[:, 0, 0:4 * 2 * NC].rearrange("p (k n) -> p k n", k=4), ACT.Silu)\
                        .then_inc(hid_act, 1)
                else:
                    for g in range(2):
                        act.activation(hidT8[:, :, 4 * g:4 * g + 4, :],
                                       src[:, :, g:g + 1, :].to_broadcast([P, 4, 4, NC]), ACT.Silu).then_inc(hid_act, 1)

            def exps(u):
                for t in range(TT):
                    act.wait_ge(max_ready, TT * u + t + 1)
                    for i in range(4):
                        src = S[:, 0, i * P:(i + 1) * P] if t == 0 else \
                            S[:, 1 + i // 2, (i % 2) * SEQ:(i % 2 + 1) * SEQ]
                        act.activation((e0 if t == 0 else e1)[:, i, :], src, ACT.Exp,
                                       bias=nmax[:, 4 * t + i:4 * t + i + 1],
                                       accum_out=sums[:, 4 * t + i:4 * t + i + 1]).then_inc(exp_done, 1)

            def take_pT(u):
                w = NB if u < N_A else NB // 2
                if u:
                    act.wait_ge(pv_done, TT * u)
                for k in range(3):
                    act.wait_ge(probs_turned, 3 * u + k + 1)
                    act.activation(pT[:, k, 0:w], S[:, k, 0:w], ACT.Copy).then_inc(pT_ready, 1)

            def take_oa(g):
                for t in range(TT):
                    act.wait_ge(pv_done, TT * (2 * g + 1) + t + 1)
                    act.activation(oaT[:, t, 4 * g:4 * g + 4, :], O[:, t, :].rearrange("p (h q) -> p h q", h=4),
                                   ACT.Copy).then_inc(o_taken, 1)

            def square_ob(u):
                for t in range(TT):
                    act.wait_ge(pv_done, TT * u + t + 1)
                    for h in range(2):
                        j = 2 * t + h
                        if u > N_A and j == 0:
                            act.wait_ge(ob_squared, 4 * (u - N_A))
                            act.wait_ge(ob_rstd, u - N_A)
                        act.activation(junk[:, t, h * SEQ:(h + 1) * SEQ], O[:, t, h * SEQ:(h + 1) * SEQ], ACT.Square,
                                       accum_out=ssb[:, j:j + 1]).then_inc(ob_squared, 1)

            def silu_z(b):
                k = b - 11
                for t in range(TT):
                    a = use_done(b, t)
                    if k:
                        act.wait_ge(z_turned, TT * (k - 1) + t + 1)
                    act.activation(stage[:, t, :], a[:, :], ACT.Silu, scale=rstd[:, t:t + 1])\
                        .then_inc(acc_read["s"], 1)

            def mix_hi_part(b):
                k = b - 11
                for t in range(TT):
                    d = mixT[k // 2][0][:, 4 * (k % 2):4 * (k % 2) + 4, t * P:(t + 1) * P]
                    if k < 2:
                        act.wait_ge(mix_f, TT * k + t + 1)
                        src = stage2[:, t, :]
                    else:
                        act.wait_ge(z_turned, TT * k + t + 1)
                        src = S[:, t, :]
                    act.activation(d, src.rearrange("p (h q) -> p h q", h=4), ACT.Copy).then_inc(mix_hi, 1)

            def square_y(n):
                for t in range(TT):
                    act.wait_ge(acc_read["v"], reads("v", TT * (N_IN + n) + t + 1))
                    if n:
                        act.wait_ge(y_squared, TT * (n - 1) + t + 1)
                    else:
                        act.wait_ge(ob_squared, 8)
                    act.activation(junk[:, t, :], x_nat[:, t, n * NB:(n + 1) * NB], ACT.Square,
                                   accum_out=ssy[:, 4 * t + n:4 * t + n + 1]).then_inc(y_squared, 1)

            h_hi_part(0)
            split_hi(0)
            act.dma_start(const[:, :], consts).then_inc(const_in, 16)
            act.dma_start(posT[:, :], cmp_pos).then_inc(const_in, 16)
            act.dma_start(x_nat[:, :, :], x.rearrange("(t p) d -> p t d", p=P)).then_inc(x_in, 16)
            h_hi_part(1)
            split_hi(1)
            act.dma_start(gwf[:, :, :], w_gate).then_inc(gw_in, 16)
            act.dma_start(w2["ck"][:, :, :], ck_w2).then_inc(w2_in, 16)
            act.dma_start(w2["cv"][:, :, :], cv_w2).then_inc(w2_in, 16)
            act.dma_start(lamv[:, :, :], lam.partition_broadcast(P)).then_inc(lam_in, 16)
            for c in range(N_CHUNKS):
                if c + 2 < N_CHUNKS:
                    if c + 2 < 4:
                        h_hi_part(c + 2)
                    split_hi(c + 2)
                if c == 1:
                    act.wait_ge(x_in, 16)
                    for t in range(TT):
                        if t:
                            act.wait_ge(x_squared, t)
                        act.activation(sq[:, :], x_nat[:, t, :], ACT.Square, accum_out=ssq[:, t:t + 1])\
                            .then_inc(x_squared, 1)
                    act.wait_ge(rstd_steps, 2)
                if c == 4:
                    take_vc()
                if c == 6:
                    take_heads(0)
                if c == 7:
                    for k, w in enumerate(("ck", "cv")):
                        act.wait_ge(blk_sum, k + 1)
                        act.activation(blk[w][:, 0:CMP_BLOCK * 64].rearrange("p (l s n) -> p l s n", l=CMP_BLOCK, s=2)[:, :, 0, :],
                                       blkf[w][:, :, :, :].rearrange("p l g n -> p l (g n)"), ACT.Copy).then_inc(blk_hi, 1)
                if c == 8:
                    act.wait_ge(gw_in, 16)
                    act.wait_ge(blk_zero, 5)
                    act.activation(gw[:, 0:KT * 64].rearrange("p (k j) -> p k j", k=KT)[:, :, 0:N_GATE], gwf[:, :, :],
                                   ACT.Copy).then_inc(gw_hi, 1)
                if c == 10:
                    take_heads(1)
                if c == 12:
                    act.wait_ge(g_done, 1)
                    act.activation(gT[:, :], S[0:64, 0, 0:SEQ], ACT.Copy).then_inc(g_taken, 1)
                if c == 13:
                    act.wait_ge(g_turned, 1)
                    for t in range(TT):
                        act.activation(gate[:, t, :], S[:, 1, 32 * t:32 * t + N_GATE], ACT.Exp, scale=nrstd[:, t:t + 1])\
                            .then_inc(g_exp, 1)
                    act.wait_ge(lam_sums, 1)
                    act.activation(lamd, lamd, ACT.Exp).then_inc(lam_exp, 1)
                if c == LAST["in", 2] + 1:
                    take_v(2)
                for b in (3, 4, 5, 6, 7, 8):
                    if c == HEADS_AT[b] + 1:
                        take_heads(b)
                if c == 24:
                    take_hid(0)
                if c == 25:
                    silu_hid(0)
                if c == 27:
                    act.wait_ge(cmp_out, 1)
                    act.activation(kcmpT[:, :], O[:, 0, P:P + 2 * NC], ACT.Copy).then_inc(kcmp_ready, 1)
                if c == 40:
                    take_hid(1)
                if c == 41:
                    silu_hid(1)
                if c == 44:
                    act.wait_ge(cs_shift, 1)
                    act.activation(ce[:, :, :, :], cs[:, :, :, :], ACT.Exp).then_inc(ce_done, 1)
                if c == HEADS_AT[6] + 1:
                    act.wait_ge(pc_turned, 1)
                    act.activation(pcT[:, :, :], S[:, 0, 0:SEQ].rearrange("p (t q) -> p t q", t=TT), ACT.Copy)\
                        .then_inc(pcT_ready, 1)
                for u in range(N_UNITS):
                    if c == UNIT_AT[u] + 4:
                        take_pT(u)
                    if c == UNIT_AT[u] + 1:
                        exps(u)
                if c == UNIT_AT[1] + 5:
                    take_oa(0)
                if c == UNIT_AT[3] + 5:
                    take_oa(1)
                for u in range(N_A, N_UNITS):
                    if c == UNIT_AT[u] + 5:
                        square_ob(u)
                if c == UNIT_AT[5]:
                    act.wait_ge(pv_done, TT * N_A)
                    act.dma_start(subw[:, :], subln_w.partition_broadcast(P)).then_inc(subw_in, 16)
                for b in (9, 10):
                    if c == LAST["in", b] + 1:
                        take_v(b)
                if c == 66:
                    act.wait_ge(pv_done, TT * N_UNITS)
                    act.dma_start(fw[:, :], final_w.partition_broadcast(P)).then_inc(fw_in, 16)
                for b in range(11, N_IN):
                    if c == LAST["in", b] + 1:
                        silu_z(b)
                    if c == LAST["in", b] + (2 if b == 14 else 3):
                        mix_hi_part(b)
                for n in range(N_OUT - 1):
                    if c == LAST["out", n] + 2:
                        square_y(n)
            square_y(N_OUT - 1)
            for t in range(TT):
                act.wait_ge(y_rstd, t + 1)
                act.wait_ge(yw_ready, TT * (N_OUT - 2) + t + 1)
                act.activation(x_nat[:, t, 0:D_MODEL // 2], x_nat[:, t, 0:D_MODEL // 2], ACT.Copy, scale=rsy[:, t:t + 1])\
                    .then_inc(y_out_s, 1)

        @block.vector
        def _(dve):
            def link(ins):
                link.n += 1
                ins.then_inc(vstep, 1)
                dve.wait_ge(vstep, link.n)
            link.n = 0

            def split_lo(c):
                dve.wait_ge(hi_ready, c + 1)
                dve.tensor_tensor(wlo[:, c % SPLIT, :], raw[:, c % RAW, :], whi[:, c % SPLIT, :].bitcast(f32), ALU.subtract)\
                    .then_inc(lo_ready, 1)

            def h_scale_part(i):
                dve.wait_ge(xT_in[i], 16)
                h = xTs[:, CH * i:CH * i + CH, :]
                dve.tensor_tensor(h, h, nw[:, CH * i:CH * i + CH].unsqueeze(2).to_broadcast([P, CH, SEQ]), ALU.mult)\
                    .then_inc(h_scaled, 1)

            def h_lo_part(i):
                dve.wait_ge(h_hi, i + 1)
                dve.tensor_tensor(hT[1][:, CH * i:CH * i + CH, :], xTs[:, CH * i:CH * i + CH, :],
                                  hT[0][:, CH * i:CH * i + CH, :].bitcast(f32), ALU.subtract).then_inc(h_lo, 1)

            def use_done(b, t):
                dve.wait_ge(acc_done, TT * b + t + 1)
                return acc[(TT * b + t) % 3]

            def rope(b):
                n = ROPE.index(b)
                nh = 2 if b == 0 else 4
                w = nh * HEAD
                for t in range(TT):
                    a = use_done(b, t)
                    if n:
                        dve.wait_ge(heads_turned, TT * (n - 1) + t + 1)
                    else:
                        dve.wait_ge(acc_read["s"], t + 1)
                    a4 = a[:, 0:w].rearrange("p (h s d) -> p h s d", h=nh, s=2)
                    s4 = stage2[:, t, 0:w].rearrange("p (h s d) -> p h s d", h=nh, s=2)
                    c3 = cos[:, t:t + 1, :].to_broadcast([P, 2 * nh, HEAD // 2])
                    s3 = sin[:, t:t + 1, :].to_broadcast([P, nh, HEAD // 2])
                    dve.tensor_tensor(stage[:, t, 0:w].rearrange("p (h d) -> p h d", d=HEAD // 2),
                                      a[:, 0:w].rearrange("p (h d) -> p h d", d=HEAD // 2), c3, ALU.mult)
                    dve.scalar_tensor_tensor(s4[:, :, 0, :], a4[:, :, 1, :], -1.0, s3, ALU.mult, ALU.mult)
                    dve.tensor_tensor(s4[:, :, 1, :], a4[:, :, 0, :], s3, ALU.mult)\
                        .then_inc(acc_read["v"], 1)

            def maxes(u):
                for t in range(TT):
                    dve.wait_ge(scores_done, TT * u + t + 1)
                    src = S[:, 0, :].rearrange("p (m k) -> p m k", m=4) if t == 0 else \
                        S[:, 1:3, :].rearrange("p b (m k) -> p (b m) k", m=2)
                    dve.tensor_reduce(nmax[:, 4 * t:4 * t + 4], src, AX.X, ALU.max, negate=True).then_inc(max_ready, 1)

            def weights(u):
                g, br = unit_a(u)
                dve.wait_ge(exp_done, 8 * (u + 1))
                link(dve.reciprocal(coef, sums))
                link(dve.tensor_tensor(coef.rearrange("p (t h) -> p t h", t=TT), coef.rearrange("p (t h) -> p t h", t=TT),
                                       gate[:, :, :].rearrange("p t (h b) -> p t h b", b=3)[:, :, 4 * g:4 * g + 4, br],
                                       ALU.mult))
                for t in range(TT):
                    e = e0 if t == 0 else e1
                    for i in range(4):
                        dve.tensor_scalar(e[:, i, :], e[:, i, :], coef[:, 4 * t + i:4 * t + i + 1], None, ALU.mult)\
                            .then_inc(probs_ready, 1)

            def weights_b(u):
                dve.wait_ge(exp_done, 8 * (u + 1))
                link(dve.reciprocal(coef, sums))
                c3 = coef.rearrange("p (t m h) -> p t m h", t=TT, m=2)[:, :, 1, :]
                link(dve.tensor_scalar(c3, c3, nlam, None, ALU.mult))
                for t in range(TT):
                    e = e0 if t == 0 else e1
                    for i in (2, 3):
                        last = dve.tensor_scalar(e[:, i, :], e[:, i, :], coef[:, 4 * t + i:4 * t + i + 1], None, ALU.mult)
                    link(last)
                    for i in range(2):
                        dve.scalar_tensor_tensor(e[:, i, :], e[:, i, :], coef[:, 4 * t + i:4 * t + i + 1], e[:, 2 + i, :],
                                                 ALU.mult, ALU.add).then_inc(probs_ready, 1)

            def take_ob(u):
                k = u - N_A
                dve.wait_ge(subw_in, 16)
                dve.wait_ge(ob_rstd, k + 1)
                for t in range(TT):
                    for h in range(2):
                        j = 2 * t + h
                        dve.scalar_tensor_tensor(ob[:, t, (2 * k + h) * SEQ:(2 * k + h + 1) * SEQ],
                                                 O[:, t, h * SEQ:(h + 1) * SEQ], rsb[:, j:j + 1], subw[:, :],
                                                 ALU.mult, ALU.mult).then_inc(ob_ready, 1)

            def gate_ob(b):
                k = b - 13
                dve.wait_ge(ob_ready, 8)
                for t in range(TT):
                    dve.wait_ge(acc_read["s"], reads("s", TT * b + t + 1))
                    dve.tensor_tensor(stage[:, t, :], stage[:, t, :], ob[:, t, k * NB:(k + 1) * NB], ALU.mult)\
                        .then_inc(zb_ready, 1)

            def mix_a(b):
                k = b - 11
                for t in range(TT):
                    dve.wait_ge(z_turned, TT * k + t + 1)
                    if k:
                        dve.wait_ge(mix_hi, TT * (k - 1) + t + 1)
                    dve.wait_ge(o_taken, TT * (k + 1))
                    dve.tensor_tensor(stage2[:, t, :].rearrange("p (h q) -> p h q", h=4),
                                      oaT[:, t, 4 * k:4 * k + 4, :], S[:, t, :].rearrange("p (h q) -> p h q", h=4),
                                      ALU.mult).then_inc(mix_f, 1)

            def mix_lo_part(b):
                k = b - 11
                for t in range(TT):
                    hi, lo = (m[:, 4 * (k % 2):4 * (k % 2) + 4, t * P:(t + 1) * P] for m in mixT[k // 2])
                    src = stage2[:, t, :] if k < 2 else S[:, t, :]
                    dve.wait_ge(mix_hi, TT * k + t + 1)
                    dve.tensor_tensor(lo, src.rearrange("p (h q) -> p h q", h=4), hi.bitcast(f32), ALU.subtract)\
                        .then_inc(mix_lo, 1)

            def residual(n):
                for t in range(TT):
                    a = use_done(N_IN + n, t)
                    y = x_nat[:, t, n * NB:(n + 1) * NB]
                    dve.tensor_tensor(y, a[:, :], y, ALU.add).then_inc(acc_read["v"], 1)

            dve.wait_ge(nw_in, 16)
            h_scale_part(0)
            h_scale_part(1)
            h_lo_part(0)
            split_lo(0)
            h_scale_part(2)
            h_lo_part(1)
            split_lo(1)
            h_scale_part(3)
            for c in range(N_CHUNKS):
                if c + 2 < N_CHUNKS:
                    if c + 2 < 4:
                        h_lo_part(c + 2)
                    split_lo(c + 2)
                if c == 2:
                    dve.wait_ge(rstd_steps, 2)
                    for t in range(TT):
                        for tab in (cos, sin):
                            dve.tensor_scalar(tab[:, t, :], tab[:, t, :], rstd[:, t:t + 1], None, ALU.mult)\
                                .then_inc(tables, 1)
                    dve.wait_ge(tables, 2 * TT)
                for b in ROPE:
                    if c == LAST["in", b] + 1:
                        rope(b)
                if c == 7:
                    dve.wait_ge(heads_taken, TT)
                    dve.wait_ge(blk_zero, 4)
                    for k, w in enumerate(("ck", "cv")):
                        src = bass.AP(kvcT, kvcT[:, 2 * k:2 * k + 2, :].offset,
                                      [list(kvcT[:, :, :].ap[0]), [1, CMP_BLOCK], [SEQ, 2], [CMP_STRIDE, N_CMP]])
                        dve.tensor_tensor(blkf[w][:, :, :, 0:N_CMP], src,
                                          posT[:, :].unsqueeze(2).unsqueeze(3).to_broadcast([P, CMP_BLOCK, 2, N_CMP]),
                                          ALU.add).then_inc(blk_sum, 1)
                    for k, w in enumerate(("ck", "cv")):
                        dve.wait_ge(blk_hi, k + 1)
                        b4 = blk[w][:, 0:CMP_BLOCK * 64].rearrange("p (l s n) -> p l s n", l=CMP_BLOCK, s=2)
                        dve.tensor_tensor(b4[:, :, 1, :], blkf[w][:, :, :, :].rearrange("p l g n -> p l (g n)"),
                                          b4[:, :, 0, :].bitcast(f32), ALU.subtract).then_inc(blk_lo, 1)
                if c == 9:
                    g3 = gw[:, 0:KT * 64].rearrange("p (k j) -> p k j", k=KT)
                    dve.wait_ge(gw_hi, 1)
                    dve.tensor_tensor(g3[:, :, 32:32 + N_GATE], gwf[:, :, :], g3[:, :, 0:N_GATE].bitcast(f32), ALU.subtract)\
                        .then_inc(gw_lo, 1)
                if c == 11:
                    dve.wait_ge(lam_in, 16)
                    lv = lamv[:, :, :].rearrange("p (m s) d -> p m s d", m=2)
                    link(dve.tensor_tensor(lamp[:, :, :], lv[:, :, 0, :], lv[:, :, 1, :], ALU.mult))
                    dve.tensor_reduce(lamd, lamp[:, :, :], AX.X, ALU.add).then_inc(lam_sums, 1)
                if c == 14:
                    dve.wait_ge(g_exp, TT)
                    link(dve.tensor_scalar(gate[:, :, :], gate[:, :, :], 1.0, None, ALU.add))
                    link(dve.reciprocal(gate[:, :, :], gate[:, :, :]))
                    dve.wait_ge(lam_exp, 1)
                    link(dve.scalar_tensor_tensor(nlam, lamd[:, 1:2], -LAMBDA_INIT, lamd[:, 0:1], ALU.add, ALU.subtract))
                if c == 43:
                    cst = cs[:, :, :, :].rearrange("p t h n -> p (t h) n")
                    dve.wait_ge(cs_done, 1)
                    for t in range(TT):
                        dve.tensor_tensor(cs[:, t, :, :], S[:, 0, t * P:(t + 1) * P].rearrange("p (h n) -> p h n", h=8),
                                          cadd[:, t:t + 1, :].to_broadcast([P, 8, NC]), ALU.add).then_inc(cs_masked, 1)
                    dve.wait_ge(cs_masked, TT)
                    link(dve.tensor_reduce(cstat[:, 0, :], cst[:, :, 0:N_CMP], AX.X, ALU.max))
                    dve.tensor_tensor(cst, cst, cstat[:, 0, :].unsqueeze(2).to_broadcast([P, TT * 8, NC]), ALU.subtract)\
                        .then_inc(cs_shift, 1)
                    dve.wait_ge(cmp_out, 2)
                    dve.tensor_tensor(vbd[:, :, :], O[:, 0, P:2 * P].unsqueeze(1).to_broadcast([P, 8, P]),
                                      headmask.unsqueeze(2).to_broadcast([P, 8, P]), ALU.mult).then_inc(vbd_ready, 1)
                if c == 45:
                    cet = ce[:, :, :, :].rearrange("p t h n -> p (t h) n")
                    dve.wait_ge(ce_done, 1)
                    link(dve.tensor_reduce(cstat[:, 0, :], cet[:, :, 0:N_CMP], AX.X, ALU.add))
                    link(dve.reciprocal(cstat[:, 1, :], cstat[:, 0, :]))
                    c3 = cstat[:, 1, :].rearrange("p (t h) -> p t h", t=TT)
                    link(dve.tensor_tensor(c3, c3, gate[:, :, :].rearrange("p t (h b) -> p t h b", b=3)[:, :, :, 0], ALU.mult))
                    for t in range(TT):
                        last = dve.tensor_tensor(ce[:, t, :, :], ce[:, t, :, :], c01[:, t:t + 1, :].to_broadcast([P, 8, NC]),
                                                 ALU.mult)
                    link(last)
                    dve.tensor_tensor(cet, cet, cstat[:, 1, :].unsqueeze(2).to_broadcast([P, TT * 8, NC]), ALU.mult)\
                        .then_inc(pc_ready, 1)
                for u in range(N_UNITS):
                    if c == UNIT_AT[u] + 1:
                        maxes(u)
                    if c == UNIT_AT[u] + 2:
                        (weights if u < N_A else weights_b)(u)
                for u in range(N_A, N_UNITS):
                    if c == UNIT_AT[u] + 5:
                        take_ob(u)
                for b in (11, 12):
                    if c == LAST["in", b] + 3:
                        mix_a(b)
                        mix_lo_part(b)
                for b in (13, 14):
                    if c == LAST["in", b] + 1:
                        gate_ob(b)
                    if c == LAST["in", b] + (2 if b == 14 else 3):
                        mix_lo_part(b)
                for n in range(N_OUT - 1):
                    if c == LAST["out", n] + 1:
                        residual(n)
            n = N_OUT - 1
            residual(n)
            dve.wait_ge(fw_in, 16)
            for t in range(TT):
                dve.wait_ge(y_squared, TT * n + t + 1)
                dve.tensor_reduce(ssyt[:, t:t + 1], ssy[:, 4 * t:4 * t + 4], AX.X, ALU.add).then_inc(y_sum, 1)
                y = x_nat[:, t, n * NB:(n + 1) * NB]
                link(dve.tensor_tensor(y, y, fw[:, n * NB:(n + 1) * NB], ALU.mult))
            for t in range(TT):
                dve.wait_ge(y_rstd, t + 1)
                dve.wait_ge(yw_ready, TT * (N_OUT - 2) + t + 1)
                y = x_nat[:, t, D_MODEL // 2:D_MODEL]
                dve.tensor_scalar(y, y, rsy[:, t:t + 1], None, ALU.mult).then_inc(y_out_v, 1)

        @block.tensor
        def _(pe):
            turned = {"heads": 0, "units": 0, "pT": 0}

            def products(c):
                kind, _, j = STREAM[c]
                b = block_of(c)
                s = c % SPLIT
                pe.wait_ge(hi_ready, c + 1)
                pe.wait_ge(lo_ready, c + 1)
                if kind == "in" and b == 0:
                    pe.wait_ge(h_hi, j + 1)
                    pe.wait_ge(h_lo, j + 1)
                if kind == "out":
                    pe.wait_ge(mix_hi, TT * (j + 1))
                    pe.wait_ge(mix_lo, TT * (j + 1))
                for t in range(TT):
                    n = TT * b + t
                    if j == 0 and n >= 3:
                        for e in READERS[(n - 3) // TT]:
                            pe.wait_ge(acc_read[e], reads(e, n - 2))
                    for i in range(CH):
                        k = CH * j + i
                        if kind == "in":
                            xh, xl = (h[:, k, t * P:(t + 1) * P] for h in hT)
                        else:
                            xh, xl = (m[:, k % 8, t * P:(t + 1) * P] for m in mixT[k // 8])
                        wh, wl = whi[:, s, i * NB:(i + 1) * NB], wlo[:, s, i * NB:(i + 1) * NB]
                        pe.matmul(acc[n % 3][:, :], xh, wh, start=k == 0, stop=False)
                        pe.matmul(acc[n % 3][:, :], xh, wl, start=False, stop=False)
                        last = pe.matmul(acc[n % 3][:, :], xl, wh, start=False, stop=k == KT - 1)
                    if k == KT - 1:
                        last.then_inc(acc_done, 1)
                if not ends(c):
                    last.then_inc(chunk_used, 1)

            def products_cmp(c):
                kind, _, j = STREAM[c]
                s = c % SPLIT
                k = 0 if kind == "ck" else 1
                pe.wait_ge(hi_ready, c + 1)
                pe.wait_ge(lo_ready, c + 1)
                if j == 0:
                    pe.wait_ge(blk_lo, k + 1)
                    pe.wait_ge(blk_zero, 5)
                for i in range(CH):
                    row = (CH * j + i) * 64
                    lhs = blk[kind][:, row:row + P]
                    pe.matmul(O[:, k, :], lhs, whi[:, s, i * NB:(i + 1) * NB], start=row == 0, stop=False)
                    last = pe.matmul(O[:, k, :], lhs, wlo[:, s, i * NB:(i + 1) * NB], start=False,
                                     stop=row == (CMP_BLOCK - 1) * 64)
                last.then_inc(hid_done if ends(c) else chunk_used, 1)

            def banks_free():
                if turned["heads"]:
                    pe.wait_ge(heads_taken, turned["heads"])
                if turned["units"]:
                    pe.wait_ge(exp_done, 8 * turned["units"])
                if turned["pT"]:
                    pe.wait_ge(pT_ready, 3 * turned["pT"])

            def turn_heads(b):
                n = ROPE.index(b)
                banks_free()
                if b == 0:
                    pe.wait_ge(const_in, 32)
                for t in range(TT):
                    pe.wait_ge(rope_ready, TT * n + t + 1)
                    if b == 0:
                        pe.wait_ge(acc_read["s"], t + 1)
                    for h in range(4):
                        last = pe.transpose(S[:, 1 + t, h * P:(h + 1) * P], stage[:, t, h * P:(h + 1) * P], ident)
                    last.then_inc(heads_turned, 1)
                turned["heads"] = TT * (n + 1)

            def gate_products():
                pe.wait_ge(gw_lo, 1)
                n = 0
                for k in range(KT):
                    for h in hT:
                        last = pe.matmul(S[:, 0, 0:SEQ], gw[:, k * 64:k * 64 + P], h[:, k, :], start=n == 0, stop=n == 2 * KT - 1)
                        n += 1
                last.then_inc(g_done, 1)

            def turn_gates():
                pe.wait_ge(g_taken, 1)
                banks_free()
                for t in range(TT):
                    last = pe.matmul(S[:, 1, 32 * t:32 * t + N_GATE], gT[:, t * P:(t + 1) * P], sel[:, 0:N_GATE],
                                     start=True, stop=True)
                last.then_inc(g_turned, 1)

            def turn_hid(k):
                pe.wait_ge(hid_taken, k + 1)
                if k:
                    pe.wait_ge(kcmp_ready, 1)
                for j in range(4):
                    last = pe.matmul(O[:, 0, j * 32:(j + 1) * 32], hid[:, j * P:(j + 1) * P], sel, start=True, stop=True)
                last.then_inc(hid_turned, 1)

            def cmp_keys():
                pe.wait_ge(hid_act, 1)
                pe.wait_ge(w2_in, 32)
                for j in range(4):
                    last = pe.matmul(O[:, 0, P:P + 2 * NC], w2["ck"][:, j, :], hidT[:, j, :], start=j == 0, stop=j == 3)
                last.then_inc(cmp_out, 1)

            def cmp_values():
                pe.wait_ge(hid_act, 3)
                for j in range(4):
                    last = pe.matmul(O[:, 0, P:2 * P], hidT8[:, j, :, :].rearrange("p h n -> p (h n)"), w2["cv"][:, j, :],
                                     start=j == 0, stop=j == 3)
                last.then_inc(cmp_out, 1)

            def cmp_scores():
                banks_free()
                pe.wait_ge(kcmp_ready, 1)
                for t in range(TT):
                    for h in range(8):
                        last = pe.matmul(S[:, 0, (8 * t + h) * NC:(8 * t + h + 1) * NC], qaT[:, h, t * P:(t + 1) * P],
                                         kcmpT[:, (h // 4) * NC:(h // 4 + 1) * NC], start=True, stop=True)
                last.then_inc(cs_done, 1)

            def turn_cmp():
                banks_free()
                pe.wait_ge(pc_ready, 1)
                for t in range(TT):
                    last = pe.transpose(S[:, 0, t * P:(t + 1) * P], ce[:, t, :, :].rearrange("p h n -> p (h n)"), ident)
                last.then_inc(pc_turned, 1)

            def scores(u):
                if u < N_A:
                    g, br = unit_a(u)
                    maps = [(qaT[:, 4 * g + i, :], kaT[:, 2 * (br - 1) + g, :]) for i in range(4)]
                else:
                    maps = [(qbT[:, 4 * m + 2 * (u - N_A) + h, :], kbT[:, 4 * m + 2 * (u - N_A) + h, :])
                            for m in range(2) for h in range(2)]
                banks_free()
                if u == 0:
                    pe.wait_ge(mask_ready, 3)
                for t in range(TT):
                    w = (t + 1) * P
                    for i, (q, k) in enumerate(maps):
                        dst = S[:, 0, i * P:(i + 1) * P] if t == 0 else S[:, 1 + i // 2, (i % 2) * SEQ:(i % 2 + 1) * SEQ]
                        pe.matmul(dst, q[:, t * P:(t + 1) * P], k[:, 0:w], start=True, stop=False)
                        last = pe.matmul(dst[:, t * P:w], ident16, mask16, start=False, stop=True)
                    last.then_inc(scores_done, 1)
                turned["units"] = u + 1

            def turn_probs(u):
                a = u < N_A
                banks_free()
                if u == 0:
                    pe.wait_ge(cs_masked, TT)
                if u == 1:
                    pe.wait_ge(pcT_ready, 1)
                before = sum(8 if v < N_A else 4 for v in range(u))
                for k, (t, kt) in enumerate(((0, 0), (1, 0), (1, 1))):
                    n = 4 if a else 2
                    pe.wait_ge(probs_ready, before + n * (t + 1))
                    e = e0 if t == 0 else e1
                    for i in range(n):
                        last = pe.transpose(S[:, k, i * P:(i + 1) * P], e[:, i, kt * P:(kt + 1) * P], ident)
                    last.then_inc(probs_turned, 1)
                turned["pT"] = u + 1

            def pv_a(u):
                g, br = unit_a(u)
                first, lastu = u % 2 == 0, u % 2 == 1
                if u == 0:
                    pe.wait_ge(vbd_ready, 1)
                if u == 2:
                    pe.wait_ge(o_taken, TT)
                for t in range(TT):
                    for kt in range(t + 1):
                        pe.wait_ge(pT_ready, 3 * u + t + kt + 1)
                        last = pe.matmul(O[:, t, :], va[:, kt, (2 * (br - 1) + g) * P:(2 * (br - 1) + g + 1) * P],
                                         pT[:, t + kt, :], start=first and kt == 0, stop=False)
                    if lastu:
                        pe.wait_ge(pcT_ready, 1)
                        for i in range(4):
                            last = pe.matmul(O[:, t, i * P:(i + 1) * P], vbd[:, 4 * g + i, :], pcT[:, t, :],
                                             start=False, stop=i == 3)
                    last.then_inc(pv_done, 1)

            def pv_b(u):
                k = u - N_A
                if k == 0:
                    pe.wait_ge(o_taken, 2 * TT)
                    pe.wait_ge(acc_read["s"], reads("s", TT * 10))
                else:
                    pe.wait_ge(ob_ready, 4 * k)
                    pe.wait_ge(acc_read["s"], reads("s", TT * 11))
                for t in range(TT):
                    pe.wait_ge(pT_ready, 3 * u + (1 if t == 0 else 3))
                    for h in range(2):
                        for kt in range(t + 1):
                            last = pe.matmul(O[:, t, h * SEQ:(h + 1) * SEQ], pT[:, t + kt, h * P:(h + 1) * P],
                                             vb[:, kt, (2 * k + h) * SEQ:(2 * k + h + 1) * SEQ],
                                             start=kt == 0, stop=kt == t)
                    last.then_inc(pv_done, 1)

            def turn_z(b):
                k = b - 11
                banks_free()
                if k:
                    pe.wait_ge(mix_f, TT * min(k, 2))
                if k == 3:
                    pe.wait_ge(mix_hi, TT * k)
                    pe.wait_ge(mix_lo, TT * k)
                for t in range(TT):
                    if k < 2:
                        pe.wait_ge(acc_read["s"], reads("s", TT * b + t + 1))
                    else:
                        pe.wait_ge(zb_ready, TT * (k - 2) + t + 1)
                    for h in range(4):
                        last = pe.transpose(S[:, t, h * P:(h + 1) * P], stage[:, t, h * P:(h + 1) * P], ident)
                    last.then_inc(z_turned, 1)

            for c in range(N_CHUNKS):
                (products_cmp if STREAM[c][0] in ("ck", "cv") else products)(c)
                if c == 11:
                    gate_products()
                if c == 12:
                    turn_gates()
                if c == 24:
                    turn_hid(0)
                if c == 26:
                    cmp_keys()
                if c == 40:
                    turn_hid(1)
                if c == 42:
                    cmp_values()
                    cmp_scores()
                if c == 46:
                    turn_cmp()
                for b in ROPE:
                    if c == HEADS_AT[b]:
                        turn_heads(b)
                for u in range(N_UNITS):
                    if c == UNIT_AT[u] + 3:
                        turn_probs(u)
                    if c == UNIT_AT[u] + 4:
                        (pv_a if u < N_A else pv_b)(u)
                for u in range(N_UNITS):
                    if c == UNIT_AT[u]:
                        scores(u)
                for b in range(11, N_IN):
                    if c == LAST["in", b] + (1 if b == 14 else 2):
                        turn_z(b)


def _tables():
    f = np.float32
    pos = np.arange(SEQ, dtype=f)
    inv = f(THETA) ** (-np.arange(0, HEAD, 2, dtype=f) / f(HEAD))
    ang = (pos[:, None] * inv[None, :]).astype(f)
    c = np.zeros((P, C_N), f)
    rows = lambda a: a.reshape(TT, P, -1).transpose(1, 0, 2).reshape(P, -1)
    c[:, C_COS:C_COS + 128] = rows(np.cos(ang))
    c[:, C_SIN:C_SIN + 128] = rows(np.sin(ang))
    c[:, C_ID:C_ID + P] = np.eye(P, dtype=f)
    n = np.arange(NC)
    seen = (n * CMP_STRIDE + CMP_BLOCK - 1 <= np.arange(SEQ)[:, None]) & (n < N_CMP)
    c[:, C_CADD:C_CADD + 32] = rows(np.where(seen, 0.0, NEG).astype(f))
    c[:, C_C01:C_C01 + 32] = rows(seen.astype(f))
    c[0:64, C_SEL:C_SEL + 32] = np.tile(np.eye(32, dtype=f), (2, 1))
    c[:, C_HM:C_HM + 8] = np.arange(P)[:, None] // NC == np.arange(8)
    c[:, C_HALF:C_HALF + 4] = -0.5
    return c


def kernel(x, norm_w, w_in, cmp_pos, cmp_k_w1, cmp_k_w2, cmp_v_w1, cmp_v_w2, lam_q1, lam_k1, lam_q2, lam_k2,
           subln_w, w_out, final_norm_w):
    import concourse.bacc as bacc
    from concourse.bass_utils import run_bass_kernel_spmd

    a = lambda v: np.ascontiguousarray(v)
    x, w_in, w_out = a(x)[0], a(w_in)[0], a(w_out)[0]

    def cols(name, part=None):
        at, w = COLS[name]
        return w_in[:, at:at + w] if part is None else w_in[:, at + part * NB:at + (part + 1) * NB]

    def chunks(w):
        return w.reshape(-1, CH, P, NB).transpose(0, 2, 1, 3).reshape(-1, P, CH * NB)

    parts = {("in", b): chunks(np.concatenate([cols(s[0]), cols(s[1])], axis=1) if isinstance(s[1], str) else cols(*s))
             for b, s in enumerate(BLOCKS)}
    parts["ck", 0], parts["cv", 0] = chunks(a(cmp_k_w1)[0]), chunks(a(cmp_v_w1)[0])
    parts.update({("out", n): chunks(w_out[:, n * NB:(n + 1) * NB]) for n in range(N_OUT)})
    tiles = lambda w: a(w.reshape(-1, P, w.shape[-1]).transpose(1, 0, 2))
    arrays = {
        "stream": a(np.stack([parts[k, b][j] for k, b, j in STREAM])),
        "w_gate": tiles(cols("gate")),
        "xT": tiles(x.T),
        "x_rows": a(x),
        "norm_w_t": a(a(norm_w)[0].reshape(KT, P).T),
        "cmp_pos_t": a(a(cmp_pos)[0].T),
        "ck_w2": tiles(a(cmp_k_w2)[0]),
        "cv_w2": tiles(a(cmp_v_w2)[0]),
        "lam": a(np.stack([a(v)[0] for v in (lam_q1, lam_k1, lam_q2, lam_k2)])),
        "subln": a(subln_w)[0],
        "final_w": a(final_norm_w),
        "consts": _tables(),
    }
    nc = bacc.Bacc("TRN2", target_bir_lowering=False, num_devices=1)
    args = [nc.dram_tensor(n, v.shape, mybir.dt.from_np(v.dtype), kind="ExternalInput").ap() for n, v in arrays.items()]
    res = nc.dram_tensor("result", (SEQ, D_MODEL), mybir.dt.float32, kind="ExternalOutput").ap()
    program(nc, *args, res)
    r = run_bass_kernel_spmd(nc, [arrays], core_ids=[0])
    return r.results[0]["result"].reshape(1, SEQ, D_MODEL)
```

```python
from contextlib import ExitStack

import numpy as np

import concourse.bass as bass
from concourse import mybir

P = 128
D_MODEL, SEQ, HEAD = 2048, 256, 128
TT = SEQ // P
KT = D_MODEL // P
CH = 4
NB = 512
CMP_BLOCK, CMP_STRIDE, CMP_HIDDEN = 32, 16, 512
N_CMP = (SEQ - CMP_BLOCK) // CMP_STRIDE + 1
NC = 16
SCALE = float(HEAD) ** -0.5
NEG = -1e30
NORM_EPS, SUBLN_EPS = 1e-6, 1e-5
LAMBDA_INIT = 0.8 - 0.6
THETA = 10000.0

COLS = {}
_at = 0
for _n, _w in (("qa", 1024), ("kc", 256), ("vc", 256), ("ks", 256), ("vs", 256), ("kw", 256), ("vw", 256),
               ("gate", 24), ("za", 1024), ("qb", 1024), ("kb", 1024), ("vb", 1024), ("zb", 1024)):
    COLS[_n] = (_at, _w)
    _at += _w
N_GATE = 24
BLOCKS = [("kc", "vc"), ("ks", "kw"), ("vs", "vw"), ("qa", 0), ("qa", 1), ("qb", 0), ("kb", 0), ("qb", 1),
          ("kb", 1), ("vb", 0), ("vb", 1), ("za", 0), ("za", 1), ("zb", 0), ("zb", 1)]
N_IN = len(BLOCKS)
N_OUT = D_MODEL // NB
_in = [("in", b, j) for b in range(N_IN) for j in range(KT // CH)]
_cmp = [(w, 0, j) for w in ("ck", "cv") for j in range(CMP_BLOCK // CH)]
STREAM = _in[:9]
for _i in range(16):
    STREAM += ([_in[9 + _i]] if _i < 2 else [_in[8 + _i]] if _i > 2 else []) + [_cmp[_i]]
STREAM += _in[24:]
STREAM += [("out", n, j) for n in range(N_OUT) for j in range(KT // CH)]
N_CHUNKS = len(STREAM)
LAST = {s[:2]: c for c, s in enumerate(STREAM)}

ROPE = [0, 1, 3, 4, 5, 6, 7, 8]
HEADS_AT = {0: 7, 1: 9, 3: 24, 4: 32, 5: 42, 6: 46, 7: 50, 8: 54}
GATE_AT = 11
CMP_SCORES_AT = 42
UNIT_AT = [40, 44, 48, 52, 56, 60]
N_UNITS = len(UNIT_AT)
N_A = 4
K_END, V_END = LAST["ck", 0], LAST["cv", 0]
W_PIECES = [(0, i, 1) for i in range(4)] + [(c, i, 2) for c in (1, 2, 3) for i in (0, 2)]
X_PIECES = [(0, 1), (1, 3), (4, 4), (8, 4), (12, 4)]
WARM_UP = 44
RELOAD = 72
RAW, SPLIT = 4, 3

C_COS, C_SIN, C_ID, C_CADD, C_C01, C_SEL, C_HM, C_HALF = 0, 128, 256, 384, 416, 448, 480, 488
C_N = 492


def unit_a(u):
    return u // 2, 1 + u % 2


def program(nc, stream, w_gate, xT, x, norm_w, cmp_pos, ck_w2, cv_w2, lam, subln_w, final_w, consts, out):
    f32, f32r, bf16 = mybir.dt.float32, mybir.dt.float32r, mybir.dt.bfloat16
    ALU, ACT, AX = mybir.AluOpType, mybir.ActivationFunctionType, mybir.AxisListType

    with ExitStack() as ctx:
        base = (nc.sbuf_base + 31) // 32 * 32
        top = [base]

        def region(n):
            top[0] += n
            return top[0] - n

        def sb(name, shape, dt=f32, at=None):
            n = int(np.prod(shape[1:])) * (2 if dt == bf16 else 4)
            return nc.alloc_sbuf_tensor_at(name, shape, dt, offset=region((n + 31) // 32 * 32) if at is None else at)

        r_x = region(4 * TT * D_MODEL)
        x_nat = sb("x_nat", [P, TT, D_MODEL], at=r_x)
        pT_lo = sb("pT_lo", [P, 3, NB], f32r, at=r_x)
        va_lo = sb("va_lo", [P, TT, NB], f32r, at=r_x + 4 * 3 * NB)
        hT = [sb("hT_hi", [P, KT, SEQ], f32r), sb("hT_lo", [P, KT, SEQ], f32r)]
        raw = sb("raw", [P, RAW, CH * NB])
        whi = sb("whi", [P, SPLIT, CH * NB], f32r)
        wlo = sb("wlo", [P, SPLIT, CH * NB], f32r)
        r1, r2, r3 = region(32768), region(16384), region(8192)
        r_e, r_p = region(6144), region(6144)
        r_s = region(8192)
        stage = sb("stage", [P, TT, NB], at=r_s)
        stage2 = sb("stage2", [P, TT, NB], at=r_s + 4096)
        sq = sb("sq", [P, D_MODEL], at=r_s)
        const = sb("const", [P, C_N])
        const16 = sb("const16", [P, 2 * P], bf16)
        small = sb("small", [P, 64])
        gate = sb("gate", [P, TT, N_GATE])
        kcmpT = sb("kcmpT", [P, 2 * NC])
        nw = sb("nw", [P, KT])
        BLK = CMP_BLOCK * 64 + 64
        blk = {"ck": sb("kblk", [P, BLK], f32r, at=r1), "cv": sb("vblk", [P, BLK], f32r, at=r1 + 4 * BLK)}
        r1b = r1 + 8 * BLK
        blkf = {"ck": sb("kblkf", [P, CMP_BLOCK, 2, NC], at=r1b), "cv": sb("vblkf", [P, CMP_BLOCK, 2, NC], at=r1 + 24576)}
        hid = sb("hid", [64, CMP_HIDDEN], at=r1b)
        hidT = sb("hidT", [P, 4, 2 * NC], at=r1b + 2048)
        hidT8 = sb("hidT8", [P, 4, 8, NC], at=r1b + 2560)
        gT = sb("gT", [64, SEQ], at=r1b + 4608)
        qbT = sb("qbT", [P, 8, SEQ], at=r1)
        kbT = sb("kbT", [P, 8, SEQ], at=r1 + 8192)
        vb = sb("vb_hi", [P, TT, 1024], f32r, at=r1 + 16384)
        ob = sb("ob", [P, TT, 1024], at=r1 + 24576)
        vbd = sb("vbd", [P, 8, P], at=r1 + 24576)
        pcT = sb("pcT", [P, TT, P], at=r1 + 24576 + 4096)
        cs = sb("cs", [P, TT, 8, NC], at=r1 + 24576 + 5120)
        ce = sb("ce", [P, TT, 8, NC], at=r1 + 24576 + 6144)
        fw = sb("fw", [P, D_MODEL], at=r1 + 16384)
        xTs = sb("xTs", [P, KT, SEQ], at=r2)
        qaT = sb("qaT", [P, 8, SEQ], at=r2)
        kaT = sb("kaT", [P, 4, SEQ], at=r2 + 8192)
        va = sb("va_hi", [P, TT, NB], f32r, at=r2 + 12288)
        vb_lo = sb("vb_lo", [P, TT, 1024], f32r, at=r2)
        subw = sb("subw", [P, 2 * HEAD], at=r2 + 15360)
        mixT = [[sb("mixA_hi", [P, 8, SEQ], f32r, at=r2), sb("mixA_lo", [P, 8, SEQ], f32r, at=r2 + 8192)],
                [sb("mixB_hi", [P, 8, SEQ], f32r, at=r1), sb("mixB_lo", [P, 8, SEQ], f32r, at=r1 + 8192)]]
        w2 = {"ck": sb("w2k", [P, 4, HEAD], at=r3), "cv": sb("w2v", [P, 4, HEAD], at=r3 + 2048)}
        lamv = sb("lamv", [P, 4, HEAD], at=r3 + 4096)
        lamp = sb("lamp", [P, 2, HEAD], at=r3 + 6144)
        oaT = sb("oaT", [P, TT, 8, P], at=r3)
        e0 = sb("e0", [P, 4, P], at=r_e)
        e1 = sb("e1", [P, 4, SEQ], at=r_e + 2048)
        gwf = sb("gwf", [P, KT, N_GATE], at=r_e)
        gw = sb("gw", [P, KT * 64 + 64], f32r, at=r_e + 4 * KT * N_GATE)
        pT = sb("pT_hi", [P, 3, NB], f32r, at=r_p)
        junk = sb("junk", [P, 2, NB], at=r_p)
        kvcT = sb("kvcT", [P, 4, SEQ], at=r_p)
        assert top[0] <= nc.sbuf_usable_end, (top[0], nc.sbuf_usable_end)

        cos = const[:, C_COS:C_COS + 128].rearrange("p (t d) -> p t d", t=TT)
        sin = const[:, C_SIN:C_SIN + 128].rearrange("p (t d) -> p t d", t=TT)
        ident = const[:, C_ID:C_ID + 128]
        cadd = const[:, C_CADD:C_CADD + 32].rearrange("p (t n) -> p t n", t=TT)
        c01 = const[:, C_C01:C_C01 + 32].rearrange("p (t n) -> p t n", t=TT)
        sel = const[0:64, C_SEL:C_SEL + 32]
        headmask = const[:, C_HM:C_HM + 8]
        half = const[:, C_HALF:C_HALF + 4]
        ident16, mask16 = const16[:, 0:P], const16[:, P:2 * P]
        rstd, nrstd, ssq = small[:, 0:2], small[:, 2:4], small[:, 4:6]
        nmax, sums, coef = small[:, 6:14], small[:, 14:22], small[:, 22:30]
        nlam, lamd = small[:, 30:31], small[:, 32:34]
        ssb, rsb = small[:, 34:38], small[:, 38:42]
        ssy, rsy = small[:, 42:50], small[:, 50:52]
        ssyt = small[:, 52:54]
        posT = sb("posT", [P, CMP_BLOCK])
        cstat = sb("cstat", [P, 2, TT * 8])
        assert top[0] <= nc.sbuf_usable_end, (top[0], nc.sbuf_usable_end)

        def bank(name, n=1):
            return ctx.enter_context(nc.psum_tensor(name, [P, n, NB] if n > 1 else [P, NB], f32))

        acc = [bank(f"acc{i}") for i in range(3)]
        S = bank("S", 3)
        O = bank("O", 2)

        def acc_bank(n):
            return S[:, 0, :] if n == 3 else acc[n if n < 3 else (n - 4) % 3][:, :]

        def last_use(n):
            return None if n < 4 else n - 4 if n < 7 else n - 3

        def sem(name):
            return ctx.enter_context(nc.semaphore(name))

        raw_in = [sem(f"raw_in{i}") for i in range(RAW)]
        hi_ready, lo_ready = sem("hi_ready"), sem("lo_ready")
        chunk_used = sem("chunk_used")
        xT_in = [sem(f"xT_in{i}") for i in range(len(X_PIECES))]
        w_in = [sem(f"w_in{i}") for i in range(len(W_PIECES))]
        nw_in, x_in, const_in, subw_in, fw_in, w2_in, gw_in, lam_in = (
            sem(n) for n in ("nw_in", "x_in", "const_in", "subw_in", "fw_in", "w2_in", "gw_in", "lam_in"))
        h_hi, h_lo = sem("h_hi"), sem("h_lo")
        first_hi, first_lo = sem("first_hi"), sem("first_lo")
        x_squared, rstd_steps, tables = sem("x_squared"), sem("rstd_steps"), sem("tables")
        acc_done = sem("acc_done")
        acc_read = {"v": sem("acc_read_v"), "s": sem("acc_read_s")}
        rope_ready = sem("rope_ready")
        heads_turned, heads_taken = sem("heads_turned"), sem("heads_taken")
        mask_ready = sem("mask_ready")
        blk_zero, blk_sum, blk_hi, blk_lo = sem("blk_zero"), sem("blk_sum"), sem("blk_hi"), sem("blk_lo")
        hid_done, hid_taken, hid_turned, hid_act = (sem(n) for n in ("hid_done", "hid_taken", "hid_turned", "hid_act"))
        cmp_out, kcmp_ready, vbd_ready = sem("cmp_out"), sem("kcmp_ready"), sem("vbd_ready")
        gw_hi, gw_lo, g_done, g_taken, g_turned, g_exp = (
            sem(n) for n in ("gw_hi", "gw_lo", "g_done", "g_taken", "g_turned", "g_exp"))
        lam_sums, lam_exp = sem("lam_sums"), sem("lam_exp")
        scores_done, max_ready, exp_done, probs_ready = (
            sem(n) for n in ("scores_done", "max_ready", "exp_done", "probs_ready"))
        probs_turned, pT_hi_ready, pT_lo_ready, pv_done, o_taken = (
            sem(n) for n in ("probs_turned", "pT_hi_ready", "pT_lo_ready", "pv_done", "o_taken"))
        cs_done, cs_masked, cs_shift, ce_done, pc_ready, pc_turned, pcT_ready = (
            sem(n) for n in ("cs_done", "cs_masked", "cs_shift", "ce_done", "pc_ready", "pc_turned", "pcT_ready"))
        ob_squared, ob_rstd, ob_ready = (sem(n) for n in ("ob_squared", "ob_rstd", "ob_ready"))
        zb_ready, z_turned, mix_f, mix_hi, mix_lo = (
            sem(n) for n in ("zb_ready", "z_turned", "mix_f", "mix_hi", "mix_lo"))
        y_squared, yw_ready, y_sum, y_rstd, y_out_s, y_out_v = (
            sem(n) for n in ("y_squared", "yw_ready", "y_sum", "y_rstd", "y_out_s", "y_out_v"))
        stored, vstep, pstep = sem("stored"), sem("vstep"), sem("pstep")

        READERS = {b: "v" for b in range(N_IN + N_OUT)}
        READERS.update({0: "vs", 2: "sv", 9: "sv", 10: "sv", 11: "s", 12: "s", 13: "s", 14: "s"})

        def reads(engine, uses):
            return sum(engine in READERS[n // TT] for n in range(uses))

        def values(b, t):
            at = slice(0, NB) if b == 2 else slice((b - 9) * NB, (b - 8) * NB)
            return [m[:, t, at] for m in ((va, va_lo) if b == 2 else (vb, vb_lo))]

        def block_of(c):
            kind, b, _ = STREAM[c]
            return b if kind == "in" else N_IN + b

        def ends(c):
            return c in LAST.values()

        def wait_used(eng, c):
            if c in (LAST["ck", 0], LAST["cv", 0]):
                eng.wait_ge(hid_done, 1 + (STREAM[c][0] == "cv"))
            elif ends(c):
                eng.wait_ge(acc_done, TT * (block_of(c) + 1))
            else:
                eng.wait_ge(chunk_used, sum(not ends(i) for i in range(c + 1)))

        def firsts(c, k):
            return sum(c2 < c or (c2 == c and k2 <= k) for c2, k2, n in W_PIECES if k2 + n < CH)

        block = ctx.enter_context(nc.Block())

        @block.sync
        def _(sp):
            xs = list(X_PIECES)
            for i, (c, k, n) in enumerate(W_PIECES):
                if xs and (CH * c + k == xs[0][0] or (c, k) == (0, 1)):
                    p = len(X_PIECES) - len(xs)
                    k0, n0 = xs.pop(0)
                    sp.dma_start(xTs[:, k0:k0 + n0, :], xT[:, k0:k0 + n0, :]).then_inc(xT_in[p], 16)
                sp.dma_start(raw[:, c, k * NB:(k + n) * NB], stream[c, :, k * NB:(k + n) * NB]).then_inc(w_in[i], 16)
            for i in range(RAW):
                sp.wait_ge(hi_ready, i + 1)
                sp.wait_ge(lo_ready, i + 1)
                sp.dma_start(raw[:, i, :], stream[RAW + i, :, :]).then_inc(raw_in[i], 16)
                if 1 <= i <= TT:
                    sp.dma_start(x_nat[:, i - 1, :], x[(i - 1) * P:i * P, :]).then_inc(x_in, 16)

            def load_rounds(first, end):
                with sp.Fori(first, end) as r:
                    for i in range(RAW):
                        sp.wait_ge(hi_ready, RAW * r + (i + 1 - RAW))
                        sp.wait_ge(lo_ready, RAW * r + (i + 1 - RAW))
                        sp.dma_start(raw[:, i, :], stream[bass.ds(RAW * r + i, 1)].rearrange("c p n -> (c p) n"))\
                            .then_inc(raw_in[i], 16)

            load_rounds(2, RELOAD // RAW)
            sp.wait_ge(pv_done, TT * N_UNITS)
            sp.dma_start(x_nat[:, :, :], x.rearrange("(t p) d -> p t d", p=P)).then_inc(x_in, 16)
            load_rounds(RELOAD // RAW, N_CHUNKS // RAW)
            for t in range(TT):
                for n in (1, 0, 2, 3):
                    if n:
                        sp.wait_ge(y_out_v, (N_OUT - 1) * t + n)
                    else:
                        sp.wait_ge(y_out_s, t + 1)
                    sp.dma_start(out[t * P:(t + 1) * P, n * NB:(n + 1) * NB], x_nat[:, t, n * NB:(n + 1) * NB])\
                        .then_inc(stored, 16)
            sp.wait_ge(stored, 16 * TT * N_OUT)

        @block.gpsimd
        def _(pool):
            def link(ins):
                link.n += 1
                ins.then_inc(pstep, 1)
                pool.wait_ge(pstep, link.n)
            link.n = 0

            pool.memset(const16[:, :], 0.0).then_inc(mask_ready, 1)
            pool.wait_ge(mask_ready, 1)
            pool.affine_select(out=ident16, in_=ident16, compare_op=ALU.not_equal, fill=1.0, base=0,
                               pattern=[[-1, P]], channel_multiplier=1).then_inc(mask_ready, 1)
            pool.affine_select(out=mask16, in_=mask16, compare_op=ALU.is_ge, fill=NEG, base=0,
                               pattern=[[-1, P]], channel_multiplier=1).then_inc(mask_ready, 1)
            for w in ("ck", "cv"):
                pool.memset(blkf[w][:, :, :, N_CMP:NC], 0.0).then_inc(blk_zero, 1)
                pool.memset(blk[w][:, CMP_BLOCK * 64:BLK].bitcast(f32), 0.0).then_inc(blk_zero, 1)
            pool.memset(gw[:, :].bitcast(f32), 0.0).then_inc(blk_zero, 1)

            pool.wait_ge(const_in, 32)
            pool.wait_ge(x_squared, TT)
            link(pool.tensor_scalar(ssq, ssq, 1.0 / D_MODEL, NORM_EPS, ALU.mult, ALU.add))
            pool.tensor_tensor(rstd, ssq, half[:, 0:2], ALU.pow).then_inc(rstd_steps, 1)
            pool.wait_ge(rstd_steps, 1)
            pool.tensor_scalar(nrstd, rstd, -1.0, 0.0, ALU.mult, ALU.add).then_inc(rstd_steps, 1)

            def rope_sum(b):
                w = 2 * HEAD if b == 0 else NB
                for t in range(TT):
                    pool.wait_ge(acc_read["v"], reads("v", TT * b + t + 1))
                    pool.tensor_tensor(stage[:, t, 0:w], stage[:, t, 0:w], stage2[:, t, 0:w], ALU.add)\
                        .then_inc(rope_ready, 1)

            def head_norm(u):
                k = u - N_A
                f = (1.0 - LAMBDA_INIT) ** -2
                pool.wait_ge(ob_squared, 4 * (k + 1))
                if k:
                    pool.wait_ge(ob_ready, 4 * k)
                link(pool.tensor_scalar(rsb, ssb, f / (2 * HEAD), SUBLN_EPS * f, ALU.mult, ALU.add))
                pool.tensor_tensor(rsb, rsb, half, ALU.pow).then_inc(ob_rstd, 1)

            for b in ROPE:
                rope_sum(b)
            for u in range(N_A, N_UNITS):
                head_norm(u)
            pool.wait_ge(fw_in, 16)
            for n in range(N_OUT - 1):
                for t in range(TT):
                    pool.wait_ge(acc_read["v"], reads("v", TT * (N_IN + n) + t + 1))
                    pool.wait_ge(y_squared, TT * n + t + 1)
                    y = x_nat[:, t, n * NB:(n + 1) * NB]
                    pool.tensor_tensor(y, y, fw[:, n * NB:(n + 1) * NB], ALU.mult).then_inc(yw_ready, 1)
            for t in range(TT):
                pool.wait_ge(y_sum, t + 1)
                pool.tensor_tensor(rsy[:, t:t + 1], ssyt[:, t:t + 1], half[:, 0:1], ALU.pow).then_inc(y_rstd, 1)

        @block.scalar
        def _(act):
            act.dma_start(nw[:, :], norm_w).then_inc(nw_in, 16)

            def split_hi(c):
                act.wait_ge(raw_in[c % RAW], 16 * (c // RAW))
                wait_used(act, c - SPLIT)
                act.activation(whi[:, c % SPLIT, :], raw[:, c % RAW, :], ACT.Copy).then_inc(hi_ready, 1)

            def split_hi_piece(i):
                c, k, n = W_PIECES[i]
                act.wait_ge(w_in[i], 16)
                if c >= SPLIT and k == 0:
                    wait_used(act, c - SPLIT)
                act.activation(whi[:, c % SPLIT, k * NB:(k + n) * NB], raw[:, c, k * NB:(k + n) * NB], ACT.Copy)\
                    .then_inc(hi_ready if k + n == CH else first_hi, 1)

            def h_hi_piece(k):
                act.activation(hT[0][:, k, :], xTs[:, k, :], ACT.Copy, scale=nw[:, k:k + 1]).then_inc(h_hi, 1)

            def start(c):
                for k in range(CH * c, CH * (c + 1)):
                    for p, (k0, _) in enumerate(X_PIECES):
                        if k == k0:
                            act.wait_ge(xT_in[p], 16)
                    h_hi_piece(k)
                    for i, (c2, k2, _) in enumerate(W_PIECES):
                        if CH * c2 + k2 == k:
                            split_hi_piece(i)

            def use_done(b, t):
                act.wait_ge(acc_done, TT * b + t + 1)
                return acc_bank(TT * b + t)

            def take_vc():
                for t in range(TT):
                    a = use_done(0, t)
                    act.activation(stage[:, t, NB // 2:NB], a[:, NB // 2:NB], ACT.Copy, scale=rstd[:, t:t + 1])\
                        .then_inc(acc_read["s"], 1)

            def take_v(b, t):
                a = use_done(b, t)
                dst = values(b, t)[0]
                act.activation(dst, a[:, :], ACT.Copy, scale=rstd[:, t:t + 1]).then_inc(acc_read["s"], 1)

            def take_heads(b):
                n = ROPE.index(b)
                dst = {0: kvcT[:, :, :], 1: kaT[:, :, :], 3: qaT[:, 0:4, :], 4: qaT[:, 4:8, :], 5: qbT[:, 0:4, :],
                       6: kbT[:, 0:4, :], 7: qbT[:, 4:8, :], 8: kbT[:, 4:8, :]}[b]
                for t in range(TT):
                    act.wait_ge(heads_turned, TT * n + t + 1)
                    act.activation(dst[:, :, t * P:(t + 1) * P], S[:, 1 + t, :].rearrange("p (h q) -> p h q", h=4),
                                   ACT.Copy, scale=SCALE if b in (3, 4, 5, 7) else 1.0).then_inc(heads_taken, 1)

            def take_hid(k):
                act.wait_ge(hid_done, k + 1)
                if k:
                    act.wait_ge(hid_turned, k)
                act.activation(hid[:, :], O[0:64, k, :], ACT.Copy).then_inc(hid_taken, 1)

            def silu_hid(k):
                act.wait_ge(hid_turned, k + 1)
                src = O[:, 0, 0:4 * 2 * NC].rearrange("p (k g n) -> p k g n", k=4, g=2)
                if k == 0:
                    act.activation(hidT[:, :, :], O[:, 0, 0:4 * 2 * NC].rearrange("p (k n) -> p k n", k=4), ACT.Silu)\
                        .then_inc(hid_act, 1)
                else:
                    for g in range(2):
                        act.activation(hidT8[:, :, 4 * g:4 * g + 4, :],
                                       src[:, :, g:g + 1, :].to_broadcast([P, 4, 4, NC]), ACT.Silu).then_inc(hid_act, 1)

            def exps(u):
                for t in range(TT):
                    act.wait_ge(max_ready, TT * u + t + 1)
                    for i in range(4):
                        src = S[:, 0, i * P:(i + 1) * P] if t == 0 else \
                            S[:, 1 + i // 2, (i % 2) * SEQ:(i % 2 + 1) * SEQ]
                        act.activation((e0 if t == 0 else e1)[:, i, :], src, ACT.Exp,
                                       bias=nmax[:, 4 * t + i:4 * t + i + 1],
                                       accum_out=sums[:, 4 * t + i:4 * t + i + 1]).then_inc(exp_done, 1)

            def take_pT(u):
                w = NB if u < N_A else NB // 2
                if u:
                    act.wait_ge(pv_done, TT * u)
                for k in range(3):
                    act.wait_ge(probs_turned, 3 * u + k + 1)
                    act.activation(pT[:, k, 0:w], S[:, k, 0:w], ACT.Copy).then_inc(pT_hi_ready, 1)

            def take_oa(g):
                for t in range(TT):
                    act.wait_ge(pv_done, TT * (2 * g + 1) + t + 1)
                    act.activation(oaT[:, t, 4 * g:4 * g + 4, :], O[:, t, :].rearrange("p (h q) -> p h q", h=4),
                                   ACT.Copy).then_inc(o_taken, 1)

            def square_ob(u):
                for t in range(TT):
                    act.wait_ge(pv_done, TT * u + t + 1)
                    for h in range(2):
                        j = 2 * t + h
                        if u > N_A and j == 0:
                            act.wait_ge(ob_squared, 4 * (u - N_A))
                            act.wait_ge(ob_rstd, u - N_A)
                        act.activation(junk[:, t, h * SEQ:(h + 1) * SEQ], O[:, t, h * SEQ:(h + 1) * SEQ], ACT.Square,
                                       accum_out=ssb[:, j:j + 1]).then_inc(ob_squared, 1)

            def silu_z(b, t):
                k = b - 11
                a = use_done(b, t)
                if k:
                    act.wait_ge(z_turned, TT * (k - 1) + t + 1)
                act.activation(stage[:, t, :], a[:, :], ACT.Silu, scale=rstd[:, t:t + 1])\
                    .then_inc(acc_read["s"], 1)

            def mix_hi_part(b):
                k = b - 11
                for t in range(TT):
                    d = mixT[k // 2][0][:, 4 * (k % 2):4 * (k % 2) + 4, t * P:(t + 1) * P]
                    if k < 2:
                        act.wait_ge(mix_f, TT * k + t + 1)
                        src = stage2[:, t, :]
                    else:
                        act.wait_ge(z_turned, TT * k + t + 1)
                        src = S[:, t, :]
                    act.activation(d, src.rearrange("p (h q) -> p h q", h=4), ACT.Copy).then_inc(mix_hi, 1)

            def square_y(n, t):
                act.wait_ge(acc_read["v"], reads("v", TT * (N_IN + n) + t + 1))
                if n:
                    act.wait_ge(y_squared, TT * (n - 1) + t + 1)
                else:
                    act.wait_ge(ob_squared, 8)
                act.activation(junk[:, t, :], x_nat[:, t, n * NB:(n + 1) * NB], ACT.Square,
                               accum_out=ssy[:, 4 * t + n:4 * t + n + 1]).then_inc(y_squared, 1)

            act.wait_ge(nw_in, 16)
            start(0)
            act.dma_start(const[:, :], consts).then_inc(const_in, 16)
            act.dma_start(posT[:, :], cmp_pos).then_inc(const_in, 16)
            start(1)
            def take(c, t):
                for b in (2, 9, 10):
                    if c == LAST["in", b]:
                        take_v(b, t)
                for b in range(11, N_IN):
                    if c == LAST["in", b]:
                        silu_z(b, t)

            for c in range(N_CHUNKS):
                take(c - 1, 1)
                for u in range(N_UNITS):
                    if c == UNIT_AT[u] + 4:
                        take_pT(u)
                if c + 2 < 4:
                    start(c + 2)
                elif c + 2 < N_CHUNKS:
                    split_hi(c + 2)
                if c == 4:
                    act.dma_start(gwf[:, :, :], w_gate).then_inc(gw_in, 16)
                if c == 7:
                    act.dma_start(w2["ck"][:, :, :], ck_w2).then_inc(w2_in, 16)
                    act.dma_start(w2["cv"][:, :, :], cv_w2).then_inc(w2_in, 16)
                    act.dma_start(lamv[:, :, :], lam.partition_broadcast(P)).then_inc(lam_in, 16)
                if c == 5:
                    act.wait_ge(x_in, 16 * TT)
                    for t in range(TT):
                        if t:
                            act.wait_ge(x_squared, t)
                        act.activation(sq[:, :], x_nat[:, t, :], ACT.Square, accum_out=ssq[:, t:t + 1])\
                            .then_inc(x_squared, 1)
                if c == 6:
                    act.wait_ge(rstd_steps, 2)
                    take_vc()
                if c == 8:
                    take_heads(0)
                if c == 9:
                    for k, w in enumerate(("ck", "cv")):
                        act.wait_ge(blk_sum, k + 1)
                        b4 = blk[w][:, 0:CMP_BLOCK * 64].rearrange("p (l s n) -> p l s n", l=CMP_BLOCK, s=2)
                        act.activation(b4[:, :, 0, :], blkf[w][:, :, :, :].rearrange("p l g n -> p l (g n)"), ACT.Copy)\
                            .then_inc(blk_hi, 1)
                if c == 9:
                    act.wait_ge(gw_in, 16)
                    act.wait_ge(blk_zero, 5)
                    act.activation(gw[:, 0:KT * 64].rearrange("p (k j) -> p k j", k=KT)[:, :, 0:N_GATE], gwf[:, :, :],
                                   ACT.Copy).then_inc(gw_hi, 1)
                if c == 10:
                    take_heads(1)
                if c == GATE_AT + 1:
                    act.wait_ge(g_done, 1)
                    act.activation(gT[:, :], S[0:64, 0, 0:SEQ], ACT.Copy).then_inc(g_taken, 1)
                if c == GATE_AT + 2:
                    act.wait_ge(g_turned, 1)
                    for t in range(TT):
                        act.activation(gate[:, t, :], S[:, 1, 32 * t:32 * t + N_GATE], ACT.Exp, scale=nrstd[:, t:t + 1])\
                            .then_inc(g_exp, 1)
                    act.wait_ge(lam_sums, 1)
                    act.activation(lamd, lamd, ACT.Exp).then_inc(lam_exp, 1)
                for b in (3, 4, 5, 6, 7, 8):
                    if c == HEADS_AT[b] + 1:
                        take_heads(b)
                if c == K_END + 1:
                    take_hid(0)
                if c == K_END + 2:
                    silu_hid(0)
                if c == K_END + 4:
                    act.wait_ge(cmp_out, 1)
                    act.activation(kcmpT[:, :], O[:, 0, P:P + 2 * NC], ACT.Copy).then_inc(kcmp_ready, 1)
                if c == V_END + 1:
                    take_hid(1)
                if c == V_END + 2:
                    silu_hid(1)
                if c == CMP_SCORES_AT + 2:
                    act.wait_ge(cs_shift, 1)
                    act.activation(ce[:, :, :, :], cs[:, :, :, :], ACT.Exp).then_inc(ce_done, 1)
                if c == CMP_SCORES_AT + 5:
                    act.wait_ge(pc_turned, 1)
                    act.activation(pcT[:, :, :], S[:, 0, 0:SEQ].rearrange("p (t q) -> p t q", t=TT), ACT.Copy)\
                        .then_inc(pcT_ready, 1)
                for u in range(N_UNITS):
                    if c == UNIT_AT[u] + 1:
                        exps(u)
                if c == UNIT_AT[1] + 5:
                    take_oa(0)
                if c == UNIT_AT[3] + 5:
                    take_oa(1)
                for u in range(N_A, N_UNITS):
                    if c == UNIT_AT[u] + 5:
                        square_ob(u)
                if c == UNIT_AT[5]:
                    act.wait_ge(pv_done, TT * N_A)
                    act.dma_start(subw[:, :], subln_w.partition_broadcast(P)).then_inc(subw_in, 16)
                if c == UNIT_AT[-1] + 6:
                    act.wait_ge(pv_done, TT * N_UNITS)
                    act.dma_start(fw[:, :], final_w.partition_broadcast(P)).then_inc(fw_in, 16)
                for b in range(11, N_IN):
                    if c == LAST["in", b] + (2 if b == 14 else 3):
                        mix_hi_part(b)
                for n in range(N_OUT - 1):
                    if c == LAST["out", n] + 2:
                        for t in range(TT):
                            square_y(n, t)
                take(c, 0)
            for t in range(TT):
                square_y(N_OUT - 1, t)
                act.wait_ge(y_rstd, t + 1)
                act.wait_ge(yw_ready, TT * (N_OUT - 2) + t + 1)
                act.activation(x_nat[:, t, 0:NB], x_nat[:, t, 0:NB], ACT.Copy, scale=rsy[:, t:t + 1]).then_inc(y_out_s, 1)

        @block.vector
        def _(dve):
            def link(ins):
                link.n += 1
                ins.then_inc(vstep, 1)
                dve.wait_ge(vstep, link.n)
            link.n = 0

            def split_lo(c):
                dve.wait_ge(hi_ready, c + 1)
                dve.tensor_tensor(wlo[:, c % SPLIT, :], raw[:, c % RAW, :], whi[:, c % SPLIT, :].bitcast(f32), ALU.subtract)\
                    .then_inc(lo_ready, 1)

            def start(c):
                for k in range(CH * c, CH * (c + 1)):
                    dve.wait_ge(h_hi, k + 1)
                    dve.scalar_tensor_tensor(hT[1][:, k, :], xTs[:, k, :], nw[:, k:k + 1], hT[0][:, k, :].bitcast(f32),
                                             ALU.mult, ALU.subtract).then_inc(h_lo, 1)
                    for i, (c2, k2, n) in enumerate(W_PIECES):
                        if CH * c2 + k2 == k:
                            last = k2 + n == CH
                            if last:
                                dve.wait_ge(hi_ready, c + 1)
                            else:
                                dve.wait_ge(first_hi, firsts(c, k2))
                            at = slice(k2 * NB, (k2 + n) * NB)
                            dve.tensor_tensor(wlo[:, c % SPLIT, at], raw[:, c, at], whi[:, c % SPLIT, at].bitcast(f32),
                                              ALU.subtract).then_inc(lo_ready if last else first_lo, 1)

            def use_done(b, t):
                dve.wait_ge(acc_done, TT * b + t + 1)
                return acc_bank(TT * b + t)

            def rope(b, t):
                n = ROPE.index(b)
                nh = 2 if b == 0 else 4
                w = nh * HEAD
                a = use_done(b, t)
                if n:
                    dve.wait_ge(heads_turned, TT * (n - 1) + t + 1)
                else:
                    dve.wait_ge(acc_read["s"], t + 1)
                a4 = a[:, 0:w].rearrange("p (h s d) -> p h s d", h=nh, s=2)
                s4 = stage2[:, t, 0:w].rearrange("p (h s d) -> p h s d", h=nh, s=2)
                c3 = cos[:, t:t + 1, :].to_broadcast([P, 2 * nh, HEAD // 2])
                s3 = sin[:, t:t + 1, :].to_broadcast([P, nh, HEAD // 2])
                dve.tensor_tensor(stage[:, t, 0:w].rearrange("p (h d) -> p h d", d=HEAD // 2),
                                  a[:, 0:w].rearrange("p (h d) -> p h d", d=HEAD // 2), c3, ALU.mult)
                dve.scalar_tensor_tensor(s4[:, :, 0, :], a4[:, :, 1, :], -1.0, s3, ALU.mult, ALU.mult)
                dve.tensor_tensor(s4[:, :, 1, :], a4[:, :, 0, :], s3, ALU.mult)\
                    .then_inc(acc_read["v"], 1)

            def maxes(u):
                for t in range(TT):
                    dve.wait_ge(scores_done, TT * u + t + 1)
                    dve.wait_ge(mask_ready, 3)
                    src = S[:, 0, :].rearrange("p (m k) -> p m k", m=4) if t == 0 else \
                        S[:, 1:3, :].rearrange("p b (m k) -> p (b m) k", m=2)
                    last = src[:, :, t * P:(t + 1) * P]
                    link(dve.tensor_tensor(last, last, mask16.unsqueeze(1).to_broadcast([P, 4, P]), ALU.add))
                    dve.tensor_reduce(nmax[:, 4 * t:4 * t + 4], src, AX.X, ALU.max, negate=True).then_inc(max_ready, 1)

            def take_v_lo(b, t):
                a = use_done(b, t)
                hi, lo = values(b, t)
                dve.wait_ge(acc_read["s"], reads("s", TT * b + t + 1))
                if b == 2:
                    dve.wait_ge(x_squared, TT)
                else:
                    dve.wait_ge(scores_done, TT * N_A)
                dve.scalar_tensor_tensor(lo, a[:, :], rstd[:, t:t + 1], hi.bitcast(f32), ALU.mult, ALU.subtract)\
                    .then_inc(acc_read["v"], 1)

            def take_pT_lo(u):
                w = NB if u < N_A else NB // 2
                if u:
                    dve.wait_ge(pv_done, TT * u)
                for k in range(3):
                    dve.wait_ge(pT_hi_ready, 3 * u + k + 1)
                    dve.tensor_tensor(pT_lo[:, k, 0:w], S[:, k, 0:w], pT[:, k, 0:w].bitcast(f32), ALU.subtract)\
                        .then_inc(pT_lo_ready, 1)

            def weights(u):
                g, br = unit_a(u)
                dve.wait_ge(exp_done, 8 * (u + 1))
                link(dve.reciprocal(coef, sums))
                link(dve.tensor_tensor(coef.rearrange("p (t h) -> p t h", t=TT), coef.rearrange("p (t h) -> p t h", t=TT),
                                       gate[:, :, :].rearrange("p t (h b) -> p t h b", b=3)[:, :, 4 * g:4 * g + 4, br],
                                       ALU.mult))
                for t in range(TT):
                    e = e0 if t == 0 else e1
                    for i in range(4):
                        dve.tensor_scalar(e[:, i, :], e[:, i, :], coef[:, 4 * t + i:4 * t + i + 1], None, ALU.mult)\
                            .then_inc(probs_ready, 1)

            def weights_b(u):
                dve.wait_ge(exp_done, 8 * (u + 1))
                link(dve.reciprocal(coef, sums))
                c3 = coef.rearrange("p (t m h) -> p t m h", t=TT, m=2)[:, :, 1, :]
                link(dve.tensor_scalar(c3, c3, nlam, None, ALU.mult))
                for t in range(TT):
                    e = e0 if t == 0 else e1
                    for i in (2, 3):
                        last = dve.tensor_scalar(e[:, i, :], e[:, i, :], coef[:, 4 * t + i:4 * t + i + 1], None, ALU.mult)
                    link(last)
                    for i in range(2):
                        dve.scalar_tensor_tensor(e[:, i, :], e[:, i, :], coef[:, 4 * t + i:4 * t + i + 1], e[:, 2 + i, :],
                                                 ALU.mult, ALU.add).then_inc(probs_ready, 1)

            def take_ob(u):
                k = u - N_A
                dve.wait_ge(subw_in, 16)
                dve.wait_ge(ob_rstd, k + 1)
                for t in range(TT):
                    for h in range(2):
                        j = 2 * t + h
                        dve.scalar_tensor_tensor(ob[:, t, (2 * k + h) * SEQ:(2 * k + h + 1) * SEQ],
                                                 O[:, t, h * SEQ:(h + 1) * SEQ], rsb[:, j:j + 1], subw[:, :],
                                                 ALU.mult, ALU.mult).then_inc(ob_ready, 1)

            def gate_ob(b):
                k = b - 13
                dve.wait_ge(ob_ready, 8)
                for t in range(TT):
                    dve.wait_ge(acc_read["s"], reads("s", TT * b + t + 1))
                    dve.tensor_tensor(stage[:, t, :], stage[:, t, :], ob[:, t, k * NB:(k + 1) * NB], ALU.mult)\
                        .then_inc(zb_ready, 1)

            def mix_a(b):
                k = b - 11
                for t in range(TT):
                    dve.wait_ge(z_turned, TT * k + t + 1)
                    if k:
                        dve.wait_ge(mix_hi, TT * (k - 1) + t + 1)
                    dve.wait_ge(o_taken, TT * (k + 1))
                    dve.tensor_tensor(stage2[:, t, :].rearrange("p (h q) -> p h q", h=4),
                                      oaT[:, t, 4 * k:4 * k + 4, :], S[:, t, :].rearrange("p (h q) -> p h q", h=4),
                                      ALU.mult).then_inc(mix_f, 1)

            def mix_lo_part(b):
                k = b - 11
                for t in range(TT):
                    hi, lo = (m[:, 4 * (k % 2):4 * (k % 2) + 4, t * P:(t + 1) * P] for m in mixT[k // 2])
                    src = stage2[:, t, :] if k < 2 else S[:, t, :]
                    dve.wait_ge(mix_hi, TT * k + t + 1)
                    dve.tensor_tensor(lo, src.rearrange("p (h q) -> p h q", h=4), hi.bitcast(f32), ALU.subtract)\
                        .then_inc(mix_lo, 1)

            def residual(n, t):
                a = use_done(N_IN + n, t)
                y = x_nat[:, t, n * NB:(n + 1) * NB]
                dve.tensor_tensor(y, a[:, :], y, ALU.add).then_inc(acc_read["v"], 1)

            def take(c, t):
                for b in ROPE[1:]:
                    if c == LAST["in", b]:
                        rope(b, t)
                for b in (2, 9, 10):
                    if c == LAST["in", b]:
                        take_v_lo(b, t)
                for n in range(N_OUT - 1):
                    if c == LAST["out", n]:
                        residual(n, t)

            start(0)
            start(1)
            for c in range(N_CHUNKS):
                take(c - 1, 1)
                for u in range(N_UNITS):
                    if c == UNIT_AT[u] + 4:
                        take_pT_lo(u)
                if c == 6:
                    dve.wait_ge(rstd_steps, 2)
                    dve.wait_ge(const_in, 32)
                    for t in range(TT):
                        for tab in (cos, sin):
                            dve.tensor_scalar(tab[:, t, :], tab[:, t, :], rstd[:, t:t + 1], None, ALU.mult)\
                                .then_inc(tables, 1)
                    dve.wait_ge(tables, 2 * TT)
                    for t in range(TT):
                        rope(0, t)
                if c + 2 < 4:
                    start(c + 2)
                elif c + 2 < N_CHUNKS:
                    split_lo(c + 2)
                if c + 2 == RELOAD:
                    dve.wait_ge(x_in, 16 * TT + 16)
                if c == 8:
                    dve.wait_ge(heads_taken, TT)
                    dve.wait_ge(blk_zero, 4)
                    for k, w in enumerate(("ck", "cv")):
                        src = bass.AP(kvcT, kvcT[:, 2 * k:2 * k + 2, :].offset,
                                      [list(kvcT[:, :, :].ap[0]), [1, CMP_BLOCK], [SEQ, 2], [CMP_STRIDE, N_CMP]])
                        dve.tensor_tensor(blkf[w][:, :, :, 0:N_CMP], src,
                                          posT[:, :].unsqueeze(2).unsqueeze(3).to_broadcast([P, CMP_BLOCK, 2, N_CMP]),
                                          ALU.add).then_inc(blk_sum, 1)
                    for k, w in enumerate(("ck", "cv")):
                        dve.wait_ge(blk_hi, k + 1)
                        b4 = blk[w][:, 0:CMP_BLOCK * 64].rearrange("p (l s n) -> p l s n", l=CMP_BLOCK, s=2)
                        dve.tensor_tensor(b4[:, :, 1, :], blkf[w][:, :, :, :].rearrange("p l g n -> p l (g n)"),
                                          b4[:, :, 0, :].bitcast(f32), ALU.subtract).then_inc(blk_lo, 1)
                if c == 10:
                    g3 = gw[:, 0:KT * 64].rearrange("p (k j) -> p k j", k=KT)
                    dve.wait_ge(gw_hi, 1)
                    dve.tensor_tensor(g3[:, :, 32:32 + N_GATE], gwf[:, :, :], g3[:, :, 0:N_GATE].bitcast(f32), ALU.subtract)\
                        .then_inc(gw_lo, 1)
                if c == 11:
                    dve.wait_ge(lam_in, 16)
                    lv = lamv[:, :, :].rearrange("p (m s) d -> p m s d", m=2)
                    link(dve.tensor_tensor(lamp[:, :, :], lv[:, :, 0, :], lv[:, :, 1, :], ALU.mult))
                    dve.tensor_reduce(lamd, lamp[:, :, :], AX.X, ALU.add).then_inc(lam_sums, 1)
                if c == GATE_AT + 3:
                    dve.wait_ge(g_exp, TT)
                    link(dve.tensor_scalar(gate[:, :, :], gate[:, :, :], 1.0, None, ALU.add))
                    link(dve.reciprocal(gate[:, :, :], gate[:, :, :]))
                    dve.wait_ge(lam_exp, 1)
                    link(dve.scalar_tensor_tensor(nlam, lamd[:, 1:2], -LAMBDA_INIT, lamd[:, 0:1], ALU.add, ALU.subtract))
                if c == CMP_SCORES_AT + 1:
                    cst = cs[:, :, :, :].rearrange("p t h n -> p (t h) n")
                    dve.wait_ge(cs_done, TT)
                    for t in range(TT):
                        dve.tensor_tensor(cs[:, t, :, :], S[:, 0, t * P:(t + 1) * P].rearrange("p (h n) -> p h n", h=8),
                                          cadd[:, t:t + 1, :].to_broadcast([P, 8, NC]), ALU.add).then_inc(cs_masked, 1)
                    dve.wait_ge(cs_masked, TT)
                    link(dve.tensor_reduce(cstat[:, 0, :], cst[:, :, 0:N_CMP], AX.X, ALU.max))
                    dve.tensor_tensor(cst, cst, cstat[:, 0, :].unsqueeze(2).to_broadcast([P, TT * 8, NC]), ALU.subtract)\
                        .then_inc(cs_shift, 1)
                    dve.wait_ge(cmp_out, 2)
                    dve.tensor_tensor(vbd[:, :, :], O[:, 0, P:2 * P].unsqueeze(1).to_broadcast([P, 8, P]),
                                      headmask.unsqueeze(2).to_broadcast([P, 8, P]), ALU.mult).then_inc(vbd_ready, 1)
                if c == CMP_SCORES_AT + 3:
                    cet = ce[:, :, :, :].rearrange("p t h n -> p (t h) n")
                    dve.wait_ge(ce_done, 1)
                    link(dve.tensor_reduce(cstat[:, 0, :], cet[:, :, 0:N_CMP], AX.X, ALU.add))
                    link(dve.reciprocal(cstat[:, 1, :], cstat[:, 0, :]))
                    c3 = cstat[:, 1, :].rearrange("p (t h) -> p t h", t=TT)
                    g0 = gate[:, :, :].rearrange("p t (h b) -> p t h b", b=3)[:, :, :, 0]
                    link(dve.tensor_tensor(c3, c3, g0, ALU.mult))
                    for t in range(TT):
                        last = dve.tensor_tensor(ce[:, t, :, :], ce[:, t, :, :], c01[:, t:t + 1, :].to_broadcast([P, 8, NC]),
                                                 ALU.mult)
                    link(last)
                    dve.tensor_tensor(cet, cet, cstat[:, 1, :].unsqueeze(2).to_broadcast([P, TT * 8, NC]), ALU.mult)\
                        .then_inc(pc_ready, 1)
                for u in range(N_UNITS):
                    if c == UNIT_AT[u] + 1:
                        maxes(u)
                    if c == UNIT_AT[u] + 2:
                        (weights if u < N_A else weights_b)(u)
                for u in range(N_A, N_UNITS):
                    if c == UNIT_AT[u] + 5:
                        take_ob(u)
                for b in (11, 12):
                    if c == LAST["in", b] + 3:
                        mix_a(b)
                        mix_lo_part(b)
                for b in (13, 14):
                    if c == LAST["in", b] + 1:
                        gate_ob(b)
                    if c == LAST["in", b] + (2 if b == 14 else 3):
                        mix_lo_part(b)
                take(c, 0)
            n = N_OUT - 1
            dve.wait_ge(fw_in, 16)
            for t in range(TT):
                residual(n, t)
                dve.wait_ge(y_squared, TT * n + t + 1)
                ss = ssy[:, N_OUT * t:N_OUT * (t + 1)]
                dve.tensor_scalar(ss, ss, 1.0 / D_MODEL, NORM_EPS, ALU.mult, ALU.add, accum_out=ssyt[:, t:t + 1])\
                    .then_inc(y_sum, 1)
                y = x_nat[:, t, n * NB:(n + 1) * NB]
                link(dve.tensor_tensor(y, y, fw[:, n * NB:(n + 1) * NB], ALU.mult))
                dve.wait_ge(yw_ready, TT * (N_OUT - 2) + t + 1)
                dve.wait_ge(y_rstd, t + 1)
                for n2 in range(1, N_OUT):
                    y = x_nat[:, t, n2 * NB:(n2 + 1) * NB]
                    dve.tensor_scalar(y, y, rsy[:, t:t + 1], None, ALU.mult).then_inc(y_out_v, 1)

        @block.tensor
        def _(pe):
            turned = {"heads": 0, "units": 0, "pT": 0}

            def products(c, tiles=(0, 1), after_tile=None):
                kind, _, j = STREAM[c]
                b = block_of(c)
                s = c % SPLIT
                if c < 4:
                    return first_products(c)
                pe.wait_ge(hi_ready, c + 1)
                pe.wait_ge(lo_ready, c + 1)
                if kind == "out":
                    pe.wait_ge(mix_hi, TT * (j + 1))
                    pe.wait_ge(mix_lo, TT * (j + 1))
                for t in tiles:
                    n = TT * b + t
                    if j == 0 and last_use(n) is not None:
                        for e in READERS[last_use(n) // TT]:
                            pe.wait_ge(acc_read[e], reads(e, last_use(n) + 1))
                    for i in range(CH):
                        k = CH * j + i
                        if kind == "in":
                            xh, xl = (h[:, k, t * P:(t + 1) * P] for h in hT)
                        else:
                            xh, xl = (m[:, k % 8, t * P:(t + 1) * P] for m in mixT[k // 8])
                        wh, wl = whi[:, s, i * NB:(i + 1) * NB], wlo[:, s, i * NB:(i + 1) * NB]
                        pe.matmul(acc_bank(n), xh, wh, start=k == 0, stop=False)
                        pe.matmul(acc_bank(n), xh, wl, start=False, stop=False)
                        last = pe.matmul(acc_bank(n), xl, wh, start=False, stop=k == KT - 1)
                    if k == KT - 1:
                        last.then_inc(acc_done, 1)
                    elif t == tiles[-1]:
                        last.then_inc(chunk_used, 1)
                    if after_tile:
                        after_tile(t)

            def first_products(c):
                for i in range(CH):
                    k = CH * c + i
                    pe.wait_ge(h_hi, k + 1)
                    pe.wait_ge(h_lo, k + 1)
                    for c2, k2, n in W_PIECES:
                        if (c2, k2) == (c, i):
                            last = k2 + n == CH
                            pe.wait_ge(hi_ready if last else first_hi, c + 1 if last else firsts(c, k2))
                            pe.wait_ge(lo_ready if last else first_lo, c + 1 if last else firsts(c, k2))
                    wh, wl = (w[:, c % SPLIT, i * NB:(i + 1) * NB] for w in (whi, wlo))
                    for t in range(TT):
                        xh, xl = (h[:, k, t * P:(t + 1) * P] for h in hT)
                        pe.matmul(acc_bank(t), xh, wh, start=k == 0, stop=False)
                        pe.matmul(acc_bank(t), xh, wl, start=False, stop=False)
                        mm = pe.matmul(acc_bank(t), xl, wh, start=False, stop=k == KT - 1)
                        if k == KT - 1:
                            mm.then_inc(acc_done, 1)
                if not ends(c):
                    mm.then_inc(chunk_used, 1)

            def products_cmp(c):
                kind, _, j = STREAM[c]
                s = c % SPLIT
                k = 0 if kind == "ck" else 1
                pe.wait_ge(hi_ready, c + 1)
                pe.wait_ge(lo_ready, c + 1)
                if j == 0:
                    pe.wait_ge(blk_lo, k + 1)
                    pe.wait_ge(blk_zero, 5)
                for i in range(CH):
                    row = (CH * j + i) * 64
                    lhs = blk[kind][:, row:row + P]
                    pe.matmul(O[:, k, :], lhs, whi[:, s, i * NB:(i + 1) * NB], start=row == 0, stop=False)
                    last = pe.matmul(O[:, k, :], lhs, wlo[:, s, i * NB:(i + 1) * NB], start=False,
                                     stop=row == (CMP_BLOCK - 1) * 64)
                last.then_inc(hid_done if ends(c) else chunk_used, 1)

            def banks_free():
                if turned["heads"]:
                    pe.wait_ge(heads_taken, turned["heads"])
                if turned["units"]:
                    pe.wait_ge(exp_done, 8 * turned["units"])
                if turned["pT"]:
                    pe.wait_ge(pT_lo_ready, 3 * turned["pT"])

            def turn_heads(b):
                n = ROPE.index(b)
                banks_free()
                if b == 0:
                    pe.wait_ge(const_in, 32)
                for t in range(TT):
                    pe.wait_ge(rope_ready, TT * n + t + 1)
                    if b == 0:
                        pe.wait_ge(acc_read["s"], t + 1)
                    for h in range(4):
                        last = pe.transpose(S[:, 1 + t, h * P:(h + 1) * P], stage[:, t, h * P:(h + 1) * P], ident)
                    last.then_inc(heads_turned, 1)
                turned["heads"] = TT * (n + 1)

            def gate_products():
                pe.wait_ge(gw_lo, 1)
                pe.wait_ge(acc_read["v"], reads("v", 4))
                n = 0
                for k in range(KT):
                    for h in hT:
                        last = pe.matmul(S[:, 0, 0:SEQ], gw[:, k * 64:k * 64 + P], h[:, k, :],
                                         start=n == 0, stop=n == 2 * KT - 1)
                        n += 1
                last.then_inc(g_done, 1)

            def turn_gates():
                pe.wait_ge(g_taken, 1)
                banks_free()
                for t in range(TT):
                    last = pe.matmul(S[:, 1, 32 * t:32 * t + N_GATE], gT[:, t * P:(t + 1) * P], sel[:, 0:N_GATE],
                                     start=True, stop=True)
                last.then_inc(g_turned, 1)

            def turn_hid(k):
                pe.wait_ge(hid_taken, k + 1)
                if k:
                    pe.wait_ge(kcmp_ready, 1)
                for j in range(4):
                    last = pe.matmul(O[:, 0, j * 32:(j + 1) * 32], hid[:, j * P:(j + 1) * P], sel, start=True, stop=True)
                last.then_inc(hid_turned, 1)

            def cmp_keys():
                pe.wait_ge(hid_act, 1)
                pe.wait_ge(w2_in, 32)
                for j in range(4):
                    last = pe.matmul(O[:, 0, P:P + 2 * NC], w2["ck"][:, j, :], hidT[:, j, :], start=j == 0, stop=j == 3)
                last.then_inc(cmp_out, 1)

            def cmp_values():
                pe.wait_ge(hid_act, 3)
                for j in range(4):
                    last = pe.matmul(O[:, 0, P:2 * P], hidT8[:, j, :, :].rearrange("p h n -> p (h n)"), w2["cv"][:, j, :],
                                     start=j == 0, stop=j == 3)
                last.then_inc(cmp_out, 1)

            def cmp_scores(t):
                if t == 0:
                    banks_free()
                    pe.wait_ge(kcmp_ready, 1)
                for h in range(8):
                    last = pe.matmul(S[:, 0, (8 * t + h) * NC:(8 * t + h + 1) * NC], qaT[:, h, t * P:(t + 1) * P],
                                     kcmpT[:, (h // 4) * NC:(h // 4 + 1) * NC], start=True, stop=True)
                last.then_inc(cs_done, 1)

            def turn_cmp():
                banks_free()
                pe.wait_ge(pc_ready, 1)
                for t in range(TT):
                    last = pe.transpose(S[:, 0, t * P:(t + 1) * P], ce[:, t, :, :].rearrange("p h n -> p (h n)"), ident)
                last.then_inc(pc_turned, 1)

            def scores(u):
                if u < N_A:
                    g, br = unit_a(u)
                    maps = [(qaT[:, 4 * g + i, :], kaT[:, 2 * (br - 1) + g, :]) for i in range(4)]
                else:
                    maps = [(qbT[:, 4 * m + 2 * (u - N_A) + h, :], kbT[:, 4 * m + 2 * (u - N_A) + h, :])
                            for m in range(2) for h in range(2)]
                banks_free()
                for t in range(TT):
                    w = (t + 1) * P
                    for i, (q, k) in enumerate(maps):
                        dst = S[:, 0, i * P:(i + 1) * P] if t == 0 else S[:, 1 + i // 2, (i % 2) * SEQ:(i % 2 + 1) * SEQ]
                        last = pe.matmul(dst, q[:, t * P:(t + 1) * P], k[:, 0:w], start=True, stop=True)
                    last.then_inc(scores_done, 1)
                turned["units"] = u + 1

            def turn_probs(u):
                a = u < N_A
                banks_free()
                if u == 0:
                    pe.wait_ge(cs_masked, TT)
                if u == 1:
                    pe.wait_ge(pcT_ready, 1)
                before = sum(8 if v < N_A else 4 for v in range(u))
                for k, (t, kt) in enumerate(((0, 0), (1, 0), (1, 1))):
                    n = 4 if a else 2
                    pe.wait_ge(probs_ready, before + n * (t + 1))
                    e = e0 if t == 0 else e1
                    for i in range(n):
                        last = pe.transpose(S[:, k, i * P:(i + 1) * P], e[:, i, kt * P:(kt + 1) * P], ident)
                    last.then_inc(probs_turned, 1)
                turned["pT"] = u + 1

            def pv_a(u):
                g, br = unit_a(u)
                first, lastu = u % 2 == 0, u % 2 == 1
                if u == 0:
                    pe.wait_ge(vbd_ready, 1)
                    pe.wait_ge(acc_read["v"], reads("v", TT * 3))
                if u == 2:
                    pe.wait_ge(o_taken, TT)
                for t in range(TT):
                    for kt in range(t + 1):
                        pe.wait_ge(pT_lo_ready, 3 * u + t + kt + 1)
                        vh, vl = (v[:, kt, (2 * (br - 1) + g) * P:(2 * (br - 1) + g + 1) * P] for v in (va, va_lo))
                        pe.matmul(O[:, t, :], vh, pT[:, t + kt, :], start=first and kt == 0, stop=False)
                        pe.matmul(O[:, t, :], vh, pT_lo[:, t + kt, :], start=False, stop=False)
                        last = pe.matmul(O[:, t, :], vl, pT[:, t + kt, :], start=False, stop=False)
                    if lastu:
                        pe.wait_ge(pcT_ready, 1)
                        for i in range(4):
                            last = pe.matmul(O[:, t, i * P:(i + 1) * P], vbd[:, 4 * g + i, :], pcT[:, t, :],
                                             start=False, stop=i == 3)
                    last.then_inc(pv_done, 1)

            def pv_b(u):
                k = u - N_A
                if k == 0:
                    pe.wait_ge(o_taken, 2 * TT)
                    pe.wait_ge(acc_read["v"], reads("v", TT * 10))
                else:
                    pe.wait_ge(ob_ready, 4 * k)
                    pe.wait_ge(acc_read["v"], reads("v", TT * 11))
                for t in range(TT):
                    pe.wait_ge(pT_lo_ready, 3 * u + (1 if t == 0 else 3))
                    for h in range(2):
                        dst = O[:, t, h * SEQ:(h + 1) * SEQ]
                        for kt in range(t + 1):
                            ph, pl = (p[:, t + kt, h * P:(h + 1) * P] for p in (pT, pT_lo))
                            vh, vl = (v[:, kt, (2 * k + h) * SEQ:(2 * k + h + 1) * SEQ] for v in (vb, vb_lo))
                            pe.matmul(dst, ph, vh, start=kt == 0, stop=False)
                            pe.matmul(dst, ph, vl, start=False, stop=False)
                            last = pe.matmul(dst, pl, vh, start=False, stop=kt == t)
                    last.then_inc(pv_done, 1)

            def turn_z(b):
                k = b - 11
                banks_free()
                if k:
                    pe.wait_ge(mix_f, TT * min(k, 2))
                if k == 3:
                    pe.wait_ge(mix_hi, TT * k)
                    pe.wait_ge(mix_lo, TT * k)
                for t in range(TT):
                    if k < 2:
                        pe.wait_ge(acc_read["s"], reads("s", TT * b + t + 1))
                    else:
                        pe.wait_ge(zb_ready, TT * (k - 2) + t + 1)
                    for h in range(4):
                        last = pe.transpose(S[:, t, h * P:(h + 1) * P], stage[:, t, h * P:(h + 1) * P], ident)
                    last.then_inc(z_turned, 1)

            pe.wait_ge(mask_ready, 3)
            for i in range(WARM_UP):
                pe.matmul(acc_bank(0)[:, 0:P], ident16, mask16, start=True, stop=True)
            for c in range(N_CHUNKS - SPLIT):
                if STREAM[c][0] in ("ck", "cv"):
                    products_cmp(c)
                else:
                    products(c, after_tile=cmp_scores if c == CMP_SCORES_AT else None)
                if c == GATE_AT:
                    gate_products()
                if c == GATE_AT + 1:
                    turn_gates()
                if c == K_END + 1:
                    turn_hid(0)
                if c == K_END + 3:
                    cmp_keys()
                if c == V_END + 1:
                    turn_hid(1)
                if c == V_END + 3:
                    cmp_values()
                if c == CMP_SCORES_AT + 4:
                    turn_cmp()
                for b in ROPE:
                    if c == HEADS_AT[b]:
                        turn_heads(b)
                for u in range(N_UNITS):
                    if c == UNIT_AT[u] + 3:
                        turn_probs(u)
                    if c == UNIT_AT[u] + 4:
                        (pv_a if u < N_A else pv_b)(u)
                for u in range(N_UNITS):
                    if c == UNIT_AT[u]:
                        scores(u)
                for b in range(11, N_IN):
                    if c == LAST["in", b] + (1 if b == 14 else 2):
                        turn_z(b)
            for t in range(TT):
                for c in range(N_CHUNKS - SPLIT, N_CHUNKS):
                    products(c, (t,))


def _tables():
    f = np.float32
    pos = np.arange(SEQ, dtype=f)
    inv = f(THETA) ** (-np.arange(0, HEAD, 2, dtype=f) / f(HEAD))
    ang = (pos[:, None] * inv[None, :]).astype(f)
    c = np.zeros((P, C_N), f)
    rows = lambda a: a.reshape(TT, P, -1).transpose(1, 0, 2).reshape(P, -1)
    c[:, C_COS:C_COS + 128] = rows(np.cos(ang))
    c[:, C_SIN:C_SIN + 128] = rows(np.sin(ang))
    c[:, C_ID:C_ID + P] = np.eye(P, dtype=f)
    n = np.arange(NC)
    seen = (n * CMP_STRIDE + CMP_BLOCK - 1 <= np.arange(SEQ)[:, None]) & (n < N_CMP)
    c[:, C_CADD:C_CADD + 32] = rows(np.where(seen, 0.0, NEG).astype(f))
    c[:, C_C01:C_C01 + 32] = rows(seen.astype(f))
    c[0:64, C_SEL:C_SEL + 32] = np.tile(np.eye(32, dtype=f), (2, 1))
    c[:, C_HM:C_HM + 8] = np.arange(P)[:, None] // NC == np.arange(8)
    c[:, C_HALF:C_HALF + 4] = -0.5
    return c


def kernel(x, norm_w, w_in, cmp_pos, cmp_k_w1, cmp_k_w2, cmp_v_w1, cmp_v_w2, lam_q1, lam_k1, lam_q2, lam_k2,
           subln_w, w_out, final_norm_w):
    import concourse.bacc as bacc
    from concourse.bass_utils import run_bass_kernel_spmd

    a = lambda v: np.ascontiguousarray(v)
    x, w_in, w_out = a(x)[0], a(w_in)[0], a(w_out)[0]

    def cols(name, part=None):
        at, w = COLS[name]
        return w_in[:, at:at + w] if part is None else w_in[:, at + part * NB:at + (part + 1) * NB]

    def chunks(w):
        return w.reshape(-1, CH, P, NB).transpose(0, 2, 1, 3).reshape(-1, P, CH * NB)

    parts = {("in", b): chunks(np.concatenate([cols(s[0]), cols(s[1])], axis=1) if isinstance(s[1], str) else cols(*s))
             for b, s in enumerate(BLOCKS)}
    parts["ck", 0], parts["cv", 0] = chunks(a(cmp_k_w1)[0]), chunks(a(cmp_v_w1)[0])
    parts.update({("out", n): chunks(w_out[:, n * NB:(n + 1) * NB]) for n in range(N_OUT)})
    tiles = lambda w: a(w.reshape(-1, P, w.shape[-1]).transpose(1, 0, 2))
    arrays = {
        "stream": a(np.stack([parts[k, b][j] for k, b, j in STREAM])),
        "w_gate": tiles(cols("gate")),
        "xT": tiles(x.T),
        "x_rows": a(x),
        "norm_w_t": a(a(norm_w)[0].reshape(KT, P).T),
        "cmp_pos_t": a(a(cmp_pos)[0].T),
        "ck_w2": tiles(a(cmp_k_w2)[0]),
        "cv_w2": tiles(a(cmp_v_w2)[0]),
        "lam": a(np.stack([a(v)[0] for v in (lam_q1, lam_k1, lam_q2, lam_k2)])),
        "subln": a(subln_w)[0],
        "final_w": a(final_norm_w),
        "consts": _tables(),
    }
    nc = bacc.Bacc("TRN2", target_bir_lowering=False, num_devices=1)
    args = [nc.dram_tensor(n, v.shape, mybir.dt.from_np(v.dtype), kind="ExternalInput").ap() for n, v in arrays.items()]
    res = nc.dram_tensor("result", (SEQ, D_MODEL), mybir.dt.float32, kind="ExternalOutput").ap()
    program(nc, *args, res)
    r = run_bass_kernel_spmd(nc, [arrays], core_ids=[0])
    return r.results[0]["result"].reshape(1, SEQ, D_MODEL)
```
